# Optimizing a Trainium2 kernel written in Bass

```python
import math
import jax, jax.numpy as jnp
from jax import lax
import numpy as np

D_MODEL = 1024
BATCH = 1
SEQ = 512
DEPTH = 1
DEC_BATCH = 8
DEC_SEQ = 4
PAST_LEN = 2048
PAGE_SIZE = 128

DN_HEADS = 8
DN_DK = 128
DN_DV = 128
DN_CONV = 4
DN_CHUNK = 64
DN_QK_W = DN_HEADS * DN_DK
DN_V_W = DN_HEADS * DN_DV
DN_CONV_W = 2 * DN_QK_W + DN_V_W
SW_HEADS = 16
SW_KV_HEADS = 2
SW_GROUP = SW_HEADS // SW_KV_HEADS
SW_HD = 64
SW_Q_W = SW_HEADS * SW_HD
SW_KV_W = SW_KV_HEADS * SW_HD
WINDOW = 128
SW_BLOCK = 128
REL_BUCKETS = 32
REL_MAX_DIST = 128
N_GROUPS = 8
EXP_PER_GROUP = 8
N_EXPERTS = N_GROUPS * EXP_PER_GROUP
TOP_K = 2
D_EXPERT = 256
MOE_BLOCK = 128
EPS = 1e-6
IN_SIZES = (DN_QK_W, DN_QK_W, DN_V_W, DN_V_W, DN_HEADS, DN_HEADS, SW_Q_W, SW_KV_W, SW_KV_W, D_MODEL, D_MODEL)
D_IN = sum(IN_SIZES)

kernel_name = 'hybrid_gdn_swa_hiermoe_step'

def rmsnorm(x, w):
    xf = x.astype(jnp.float32)
    y = xf * lax.rsqrt(jnp.mean(xf * xf, axis=-1, keepdims=True) + EPS)
    return (y * w.astype(jnp.float32)).astype(x.dtype)

def l2norm(x):
    return x * lax.rsqrt(jnp.sum(x * x, axis=-1, keepdims=True) + 1e-6)

def causal_conv(u, buf, w):
    L = u.shape[1]
    full = jnp.concatenate([buf.astype(u.dtype), u], axis=1)
    out = full[:, 0:L] * w[0]
    for i in range(1, DN_CONV):
        out = out + full[:, i:i + L] * w[i]
    return jax.nn.silu(out), full[:, L:]

def gated_delta(q, k, v, beta, g, s0):
    B, L, H, _ = q.shape
    C = min(DN_CHUNK, L)
    pad = (-L) % C
    if pad:
        padw = lambda t: jnp.pad(t, [(0, 0), (0, pad)] + [(0, 0)] * (t.ndim - 2))
        q, k, v, beta, g = (padw(t) for t in (q, k, v, beta, g))
    N = (L + pad) // C

    def chunks(t):
        return jnp.moveaxis(t.reshape((B, N, C) + t.shape[2:]), 3, 1)

    qc, kc, vc, bc, gc = (chunks(t) for t in (q, k, v, beta, g))
    G = jnp.cumsum(gc, axis=-1)
    idx = jnp.arange(C)
    causal = idx[:, None] >= idx[None, :]
    strict = idx[:, None] > idx[None, :]
    gamma = jnp.exp(jnp.where(causal, G[..., :, None] - G[..., None, :], -jnp.inf))
    kb = kc * bc[..., None]
    a = jnp.where(strict, jnp.einsum('bhncd,bhnsd->bhncs', kb, kc) * gamma, 0.0) + jnp.eye(C, dtype=kc.dtype)
    solve = lambda rhs: lax.linalg.triangular_solve(a, rhs, left_side=True, lower=True, unit_diagonal=True)
    u = solve(vc * bc[..., None])
    w = solve(kb * jnp.exp(G)[..., None])
    attn = jnp.einsum('bhncd,bhnsd->bhncs', qc, kc) * gamma
    qg = qc * jnp.exp(G)[..., None]
    kd = kc * jnp.exp(G[..., -1:] - G)[..., None]
    gl = jnp.exp(G[..., -1])
    xs = tuple(jnp.moveaxis(t, 2, 0) for t in (u, w, attn, qg, kd, gl))

    def step(s, inp):
        u_i, w_i, attn_i, qg_i, kd_i, gl_i = inp
        v_new = u_i - jnp.einsum('bhcd,bhdv->bhcv', w_i, s)
        o_i = jnp.einsum('bhcd,bhdv->bhcv', qg_i, s) + jnp.einsum('bhcs,bhsv->bhcv', attn_i, v_new)
        s = s * gl_i[..., None, None] + jnp.einsum('bhcd,bhcv->bhdv', kd_i, v_new)
        return s, o_i

    s, o = lax.scan(step, s0, xs)
    o = jnp.transpose(o, (1, 0, 3, 2, 4)).reshape(B, N * C, H, -1)[:, :L]
    return o, s

def deltanet_branch(dq, dk, dv, dz, db, da, conv_buf, s0, conv_w, a_log, dt_bias, norm_w):
    f32 = jnp.float32
    B, L = dq.shape[:2]
    qkv, new_buf = causal_conv(jnp.concatenate([dq, dk, dv], axis=-1), conv_buf, conv_w)
    q = qkv[..., :DN_QK_W].astype(f32).reshape(B, L, DN_HEADS, DN_DK)
    k = qkv[..., DN_QK_W:2 * DN_QK_W].astype(f32).reshape(B, L, DN_HEADS, DN_DK)
    v = qkv[..., 2 * DN_QK_W:].astype(f32).reshape(B, L, DN_HEADS, DN_DV)
    q = l2norm(q) * DN_DK ** -0.5
    k = l2norm(k)
    beta = jax.nn.sigmoid(db.astype(f32))
    g = -jnp.exp(a_log.astype(f32)) * jax.nn.softplus(da.astype(f32) + dt_bias.astype(f32))
    o, s = gated_delta(q, k, v, beta, g, s0.astype(f32))
    z = dz.astype(f32).reshape(B, L, DN_HEADS, DN_DV)
    o = rmsnorm(o, norm_w) * jax.nn.silu(z)
    return o.reshape(B, L, DN_V_W), new_buf, s

def rel_bucket(dist):
    n = jnp.maximum(dist, 0)
    max_exact = REL_BUCKETS // 2
    large = max_exact + (jnp.log(jnp.maximum(n, 1).astype(jnp.float32) / max_exact)
                         / math.log(REL_MAX_DIST / max_exact) * (REL_BUCKETS - max_exact)).astype(jnp.int32)
    return jnp.where(n < max_exact, n, jnp.minimum(large, REL_BUCKETS - 1))

def sink_attention(q, k, v, dist, valid, sinks, rel_table):
    f32 = jnp.float32
    Q, S = dist.shape
    s = jnp.einsum('bnqkgd,bnskd->bnkgqs', q.astype(f32), k.astype(f32)) * SW_HD ** -0.5
    bias = jnp.transpose(rel_table.astype(f32)[rel_bucket(dist)], (2, 0, 1)).reshape(SW_KV_HEADS, SW_GROUP, Q, S)
    s = jnp.where(valid[None, :, None, None], s + bias, -jnp.inf)
    sink = sinks.astype(f32).reshape(1, 1, SW_KV_HEADS, SW_GROUP, 1, 1)
    m = jnp.maximum(jnp.max(s, axis=-1, keepdims=True), sink)
    p = jnp.exp(s - m)
    p = p / (jnp.sum(p, axis=-1, keepdims=True) + jnp.exp(sink - m))
    return jnp.einsum('bnkgqs,bnskd->bnqkgd', p, v.astype(f32))

def swa_prompt(q, k, v, sinks, rel_table):
    B, L = q.shape[:2]
    nb = L // SW_BLOCK
    qb = q.reshape(B, nb, SW_BLOCK, SW_KV_HEADS, SW_GROUP, SW_HD)
    kb = k.reshape(B, nb, SW_BLOCK, SW_KV_HEADS, SW_HD)
    vb = v.reshape(B, nb, SW_BLOCK, SW_KV_HEADS, SW_HD)
    shift = lambda t: jnp.concatenate([jnp.zeros_like(t[:, :1]), t[:, :-1]], axis=1)
    kk = jnp.concatenate([shift(kb), kb], axis=2)
    vv = jnp.concatenate([shift(vb), vb], axis=2)
    kpos = jnp.arange(2 * SW_BLOCK) - SW_BLOCK
    qpos = jnp.arange(SW_BLOCK)
    dist = qpos[:, None] - kpos[None, :]
    blk_start = jnp.arange(nb) * SW_BLOCK
    valid = (((dist >= 0) & (dist < WINDOW))[None]
             & ((blk_start[:, None, None] + kpos[None, None, :]) >= 0))
    o = sink_attention(qb, kk, vv, dist, valid, sinks, rel_table)
    return o.reshape(B, L, SW_Q_W)

def swa_step(q, k_all, v_all, sinks, rel_table):
    B, Lq = q.shape[:2]
    S = k_all.shape[1]
    qpos = (S - Lq) + jnp.arange(Lq)
    dist = qpos[:, None] - jnp.arange(S)[None, :]
    valid = ((dist >= 0) & (dist < WINDOW))[None]
    o = sink_attention(q[:, None], k_all[:, None], v_all[:, None], dist, valid, sinks, rel_table)
    return o.reshape(B, Lq, SW_Q_W)

def hier_moe(h, w_rg, b_rg, w_re, b_re, w_gate, w_up, w_down):
    f32 = jnp.float32
    B, L, D = h.shape
    hf = h.reshape(-1, D)
    T = hf.shape[0]
    gprob = jax.nn.softmax((hf @ w_rg).astype(f32) + b_rg.astype(f32), axis=-1)
    gval, gidx = lax.top_k(gprob, 1)
    grp = gidx[:, 0]
    elog_all = ((hf @ w_re).astype(f32) + b_re.astype(f32)).reshape(T, N_GROUPS, EXP_PER_GROUP)
    elog = jnp.take_along_axis(elog_all, grp[:, None, None], axis=1)[:, 0]
    top_v, top_i = lax.top_k(elog, TOP_K)
    wts = jax.nn.softmax(top_v, axis=-1) * gval
    eidx = grp[:, None] * EXP_PER_GROUP + top_i
    A = T * TOP_K
    e_flat = eidx.reshape(-1)
    order = jnp.argsort(e_flat)
    e_sorted = e_flat[order]
    tok_sorted = (order // TOP_K).astype(jnp.int32)
    w_sorted = wts.reshape(-1)[order]
    counts = jnp.bincount(e_flat, length=N_EXPERTS)
    padded = ((counts + MOE_BLOCK - 1) // MOE_BLOCK) * MOE_BLOCK
    pad_end = jnp.cumsum(padded)
    pad_start = pad_end - padded
    start = jnp.cumsum(counts) - counts
    dest = pad_start[e_sorted] + (jnp.arange(A) - start[e_sorted])
    NB = -(-A // MOE_BLOCK) + N_EXPERTS
    R = NB * MOE_BLOCK
    slot_tok = jnp.full((R,), T, dtype=jnp.int32).at[dest].set(tok_sorted)
    slot_w = jnp.zeros((R,), f32).at[dest].set(w_sorted)
    block_expert = jnp.minimum(jnp.searchsorted(pad_end, jnp.arange(NB) * MOE_BLOCK, side='right'), N_EXPERTS - 1)
    xb = jnp.concatenate([hf, jnp.zeros((1, D), hf.dtype)], axis=0)[slot_tok].reshape(NB, MOE_BLOCK, D)

    def expert_block(args):
        xi, e = args
        return (jax.nn.silu(xi @ w_gate[e]) * (xi @ w_up[e])) @ w_down[e]

    yb = lax.map(expert_block, (xb, block_expert)).reshape(R, D)
    y = jax.ops.segment_sum(yb.astype(f32) * slot_w[:, None], slot_tok, num_segments=T + 1)[:T]
    return y.reshape(B, L, D).astype(h.dtype)

def hybrid_layer(x, conv_buf, dn_state, kv_prev, w_in, conv_w, a_log, dt_bias, dn_norm_w, sinks, rel_bias,
                 w_out, norm_mix_w, norm_ffn_w, w_rg, b_rg, w_re, b_re, w_gate, w_up, w_down):
    B, L, _ = x.shape
    h = rmsnorm(x, norm_mix_w)
    proj = h @ w_in
    offsets = np.cumsum(IN_SIZES)[:-1].tolist()
    dq, dk, dv, dz, db, da, sq, sk, sv, gate_a, gate_b = jnp.split(proj, offsets, axis=-1)
    o_a, new_conv, new_dn = deltanet_branch(dq, dk, dv, dz, db, da, conv_buf, dn_state,
                                            conv_w, a_log, dt_bias, dn_norm_w)
    sq = sq.reshape(B, L, SW_KV_HEADS, SW_GROUP, SW_HD)
    sk = sk.reshape(B, L, SW_KV_HEADS, SW_HD)
    sv = sv.reshape(B, L, SW_KV_HEADS, SW_HD)
    if kv_prev is None:
        o_b = swa_prompt(sq, sk, sv, sinks, rel_bias)
        keep = min(WINDOW, L)
        new_k, new_v = sk[:, L - keep:], sv[:, L - keep:]
    else:
        k_prev, v_prev = kv_prev
        k_all = jnp.concatenate([k_prev.astype(sk.dtype), sk], axis=1)
        v_all = jnp.concatenate([v_prev.astype(sv.dtype), sv], axis=1)
        o_b = swa_step(sq, k_all, v_all, sinks, rel_bias)
        keep = k_prev.shape[1]
        new_k, new_v = k_all[:, -keep:], v_all[:, -keep:]
    f32 = jnp.float32
    mixed = (jax.nn.sigmoid(gate_a.astype(f32)) * o_a + jax.nn.sigmoid(gate_b.astype(f32)) * o_b).astype(x.dtype)
    x = x + mixed @ w_out
    x = x + hier_moe(rmsnorm(x, norm_ffn_w), w_rg, b_rg, w_re, b_re, w_gate, w_up, w_down)
    return x, new_conv, new_dn, new_k, new_v

def setup_inputs(seed: int = 0) -> dict:
    key = jax.random.key(seed)
    ks = jax.random.split(key, 24)
    f32 = jnp.float32
    nrm = lambda k, shape, scale: jax.random.normal(k, shape, f32) * scale
    win_buf = min(WINDOW, PAST_LEN)
    dt = jnp.exp(jax.random.uniform(ks[9], (DEPTH, DN_HEADS), f32, math.log(1e-3), math.log(1e-1)))
    return {
        'x_prompt': nrm(ks[0], (BATCH, SEQ, D_MODEL), 1.0),
        'x_sample': nrm(ks[1], (DEC_BATCH, DEC_SEQ, D_MODEL), 1.0),
        'state_dn_conv': nrm(ks[2], (DEPTH, DEC_BATCH, DN_CONV - 1, DN_CONV_W), 1.0),
        'state_dn': nrm(ks[3], (DEPTH, DEC_BATCH, DN_HEADS, DN_DK, DN_DV), 0.1),
        'cache_swa_k': nrm(ks[4], (DEPTH, DEC_BATCH, win_buf, SW_KV_HEADS, SW_HD), 1.0),
        'cache_swa_v': nrm(ks[5], (DEPTH, DEC_BATCH, win_buf, SW_KV_HEADS, SW_HD), 1.0),
        'w_in': nrm(ks[6], (DEPTH, D_MODEL, D_IN), D_MODEL ** -0.5),
        'conv_w': nrm(ks[7], (DEPTH, DN_CONV, DN_CONV_W), DN_CONV ** -0.5),
        'a_log': jnp.log(jax.random.uniform(ks[8], (DEPTH, DN_HEADS), f32, 1.0, 16.0)),
        'dt_bias': dt + jnp.log(-jnp.expm1(-dt)),
        'dn_norm_w': 1.0 + nrm(ks[10], (DEPTH, DN_DV), 0.02),
        'sinks': nrm(ks[11], (DEPTH, SW_HEADS), 0.5),
        'rel_bias': nrm(ks[12], (REL_BUCKETS, SW_HEADS), 0.1),
        'w_out': nrm(ks[13], (DEPTH, D_MODEL, D_MODEL), D_MODEL ** -0.5),
        'norm_mix_w': 1.0 + nrm(ks[14], (DEPTH, D_MODEL), 0.02),
        'norm_ffn_w': 1.0 + nrm(ks[15], (DEPTH, D_MODEL), 0.02),
        'w_router_group': nrm(ks[16], (DEPTH, D_MODEL, N_GROUPS), D_MODEL ** -0.5),
        'b_router_group': nrm(ks[17], (DEPTH, N_GROUPS), 0.01),
        'w_router_expert': nrm(ks[18], (DEPTH, D_MODEL, N_EXPERTS), D_MODEL ** -0.5),
        'b_router_expert': nrm(ks[19], (DEPTH, N_EXPERTS), 0.01),
        'w_gate': nrm(ks[20], (DEPTH, N_EXPERTS, D_MODEL, D_EXPERT), D_MODEL ** -0.5),
        'w_up': nrm(ks[21], (DEPTH, N_EXPERTS, D_MODEL, D_EXPERT), D_MODEL ** -0.5),
        'w_down': nrm(ks[22], (DEPTH, N_EXPERTS, D_EXPERT, D_MODEL), D_EXPERT ** -0.5),
        'norm_final_w': 1.0 + nrm(ks[23], (D_MODEL,), 0.02),
    }

def reference(x_prompt, x_sample, state_dn_conv, state_dn, cache_swa_k, cache_swa_v, w_in, conv_w, a_log, dt_bias,
              dn_norm_w, sinks, rel_bias, w_out, norm_mix_w, norm_ffn_w, w_router_group, b_router_group,
              w_router_expert, b_router_expert, w_gate, w_up, w_down, norm_final_w):
    xp, xs = x_prompt, x_sample
    bp = xp.shape[0]
    p_conv, p_dn, p_k, p_v = [], [], [], []
    s_conv, s_dn, s_k, s_v = [], [], [], []
    for l in range(DEPTH):
        params = (w_in[l], conv_w[l], a_log[l], dt_bias[l], dn_norm_w[l], sinks[l], rel_bias,
                  w_out[l], norm_mix_w[l], norm_ffn_w[l], w_router_group[l], b_router_group[l],
                  w_router_expert[l], b_router_expert[l], w_gate[l], w_up[l], w_down[l])
        conv0 = jnp.zeros((bp, DN_CONV - 1, DN_CONV_W), xp.dtype)
        dn0 = jnp.zeros((bp, DN_HEADS, DN_DK, DN_DV), jnp.float32)
        xp, c, s, k, v = hybrid_layer(xp, conv0, dn0, None, *params)
        p_conv.append(c.astype(xp.dtype)); p_dn.append(s.astype(xp.dtype))
        p_k.append(k.astype(xp.dtype)); p_v.append(v.astype(xp.dtype))
        xs, c, s, k, v = hybrid_layer(xs, state_dn_conv[l], state_dn[l], (cache_swa_k[l], cache_swa_v[l]), *params)
        s_conv.append(c.astype(state_dn_conv.dtype)); s_dn.append(s.astype(state_dn.dtype))
        s_k.append(k.astype(cache_swa_k.dtype)); s_v.append(v.astype(cache_swa_v.dtype))
    y_prompt = rmsnorm(xp, norm_final_w)
    y_sample = rmsnorm(xs, norm_final_w)
    return (y_prompt, y_sample, jnp.stack(p_conv), jnp.stack(p_dn), jnp.stack(p_k), jnp.stack(p_v),
            jnp.stack(s_conv), jnp.stack(s_dn), jnp.stack(s_k), jnp.stack(s_v))


_drawn_inputs = setup_inputs


def setup_inputs(seed=0):
    import zlib

    import numpy as np

    out = dict(_drawn_inputs(seed))
    spreads = {}
    factors = {'dn_norm_w': 11.364,
     'sinks': 14.253,
     'rel_bias': 4.295,
     'b_router_group': 26.384,
     'b_router_expert': 22.457,
     'norm_final_w': 8.431,
     'norm_ffn_w': 3.692}
    for name, (base, spread) in spreads.items():
        noise = np.random.default_rng([zlib.crc32(name.encode()), seed]).standard_normal(out[name].shape)
        drawn = base * np.exp(spread * noise) if base else spread * noise
        out[name] = __import__('jax').numpy.asarray(drawn.astype(out[name].dtype))
    for name, factor in factors.items():
        out[name] = (out[name] * factor).astype(out[name].dtype)
    return out
```

```python
from contextlib import ExitStack

import concourse.bass as bass
from concourse import mybir

F32 = mybir.dt.float32
I32 = mybir.dt.int32
U32 = mybir.dt.uint32
ALU = mybir.AluOpType
ACT = mybir.ActivationFunctionType
AX = mybir.AxisListType
P = 128
NEG = -1.0e30
EPS = 1e-6
LN_EXP_SET = 6


class Chain:

    def __init__(self, eng, sem):
        self.eng, self.sem, self.n, self.turn, self.per = eng, sem, 0, None, 0

    def value(self):
        return self.n if self.turn is None else self.turn * self.per + self.n

    def inc(self, ins):
        self.n += 1
        ins.then_inc(self.sem, 1)

    def step(self, ins):
        self.inc(ins)
        self.eng.wait_ge(self.sem, self.value())

    def loop(self, i, per):
        self.turn, self.per, self.at = i, per, self.n

    def end(self, turns):
        assert self.n - self.at == self.per, (self.n - self.at, self.per)
        self.turn, self.n = None, self.at + turns * self.per


def ds(i, n=1):
    return bass.ds(i, n)


def bcast(ap, axis, n, shape):
    return ap.unsqueeze(axis).to_broadcast(shape)


def program(nc, x_prompt, x_sample, conv_state, dn_state, cache_k, cache_v, w_in, conv_w, a_log, dt_bias, dn_norm_w,
            sinks, rel_bias, w_out, norm_mix_w, norm_ffn_w, w_rg, b_rg, w_re, b_re, w_gate, w_up, w_down,
            norm_final_w, rel_map, y_p, y_s, p_conv, p_dn, p_k, p_v, s_conv, s_dn, s_k, s_v):
    D = w_in.shape[0]
    KC = D // P
    TP, TS = x_prompt.shape[0], x_sample.shape[0]
    NP = TP // P
    NT = NP + 1
    T = TP + TS
    H = dn_state.shape[1]
    B = dn_state.shape[0]
    L = TS // B
    SH = sinks.shape[0]
    HD = 64
    GATE_W = H * P
    C_Z = 3 * GATE_W
    C_BA = 4 * GATE_W
    C_SQ = C_BA + 2 * H
    C_SK = C_SQ + SH * HD
    C_GA = C_SK + 4 * HD
    C_GB = C_GA + D
    NE, FE = w_gate.shape[0], w_gate.shape[2]
    CAP = 64
    OV = (2 * T - 2) // CAP
    NPAIR = NE // 2
    NBLK = NE + OV
    NS = NBLK * CAP

    rel_d = nc.dram_tensor("rel_d", (SH, P, 384), F32).ap()
    h2_d = nc.dram_tensor("h2_d", (T, D), F32).ap()
    slot_d = nc.dram_tensor("slot_d", (NS, 1), I32).ap()
    ye_d = nc.dram_tensor("ye_d", (NS, D), F32).ap()
    ye_rows = ye_d.rearrange("(p j) d -> p j d", p=P)

    with ExitStack() as ctx:
        def sb(name, shape, dt=F32):
            return ctx.enter_context(nc.sbuf_tensor(name, shape, dt))

        def sem(name):
            return ctx.enter_context(nc.semaphore(name))

        PB = [ctx.enter_context(nc.psum_tensor(f"PB{i}", [P, 512], F32)) for i in range(8)]

        ident = sb("ident", [P, P])
        ones = sb("ones", [P, P])
        m_le = sb("m_le", [P, P])
        m_gt = sb("m_gt", [P, P])
        m_ge = sb("m_ge", [P, P])
        blk = sb("blk", [TS, B, L])
        bsel = sb("bsel", [TS, B])
        s_le = sb("s_le", [TS, TS])
        s_gt = sb("s_gt", [TS, TS])
        s_ge = sb("s_ge", [TS, TS])
        eps_t = sb("eps_t", [P, 2])
        mixed = sb("mixed", [P, NT, D])
        sc = sb("sc", [P, 256])

        arena = sb("arena", [P, 37632])
        top = [0]

        def cut(*shape, parts=P):
            n = 1
            for s in shape:
                n *= s
            a = arena[0:parts, top[0]:top[0] + n]
            top[0] += n
            assert top[0] <= 37632, top[0]
            if len(shape) == 2:
                return a.rearrange("p (a b) -> p a b", a=shape[0])
            if len(shape) == 3:
                return a.rearrange("p (a b c) -> p a b c", a=shape[0], b=shape[1])
            if len(shape) == 4:
                return a.rearrange("p (a b c d) -> p a b c d", a=shape[0], b=shape[1], c=shape[2])
            return a

        hT = cut(KC, T)
        nmix = cut(KC)
        kz = cut(2, 2, TP)
        skd = cut(2, TS)
        kvrow = cut(NT, 4 * HD)
        qz = cut(B, 2, 2, 16)
        scal = cut(6, NT, H)
        glS = cut(B, H)
        graw = cut(NT, H)
        wch = cut(KC, 4, P)
        wrow = cut(KC, 3, P)
        bias = cut(SH, 256)
        sinkb = cut(SH)
        dnw = cut(P)
        sgb_s = cut(D)
        loop_at = top[0]
        cs = cut(3, P)
        cst = cut(3, 28)
        rawP = cut(3, TP + 3)
        rawS = cut(3, B, L + 3)
        co = cut(3, T)
        ex = cut(3, T)
        qk = cut(2, T)
        sqT = cut(TP)
        ct = cut(3, 27)
        crow = cut(3, P)
        hsc = cut(6, NT)
        hgl = cut(B)
        gm = cut(NP, P)
        E = cut(NP, P)
        Es = cut(NP, P)
        Et = cut(NP, P)
        Rv = cut(NP, P)
        Rk = cut(NP, P)
        kd = cut(NP, P)
        PW = cut(2, NP, P)
        PT = cut(2, NP, P)
        Tt = cut(NP, P)
        St = cut(P)
        orow = cut(NT, P)
        gates = cut(NT, 3, P)
        loop_end = top[0]
        attn = ex[:, 0, 0:512].rearrange("p (n c) -> p n c", n=NP)
        nwT = gm
        vnew = Es
        sig = sb("sig", [P, 2, 3, P])
        Sb = sb("Sb", [P, B, P])
        sm = sb("sm", [P, 2, 2, 256])
        pT = sb("pT", [P, 4, P])
        att = sb("att", [P, 2, 8])
        esk = sb("esk", [P, 2, 2])
        rinv = sb("rinv", [P, NP, 2])
        ssq = sb("ssq", [P, 3, NT])
        hbeta = sb("hbeta", [P, NT])
        sS = sb("sS", [TS, 12, P])
        Vm = sb("Vm", [TS, B, P])
        wqT = sb("wqT", [P, B, 2, L])
        wqo = sb("wqo", [P, 2, TS])
        xh = kz.rearrange("p a b c -> p (a b c)")
        biasS = sb("biasS", [P, 2, 133])
        mixer_end = top[0]

        top[0] = loop_at
        krows = cut(B, 2, 2, HD)
        vrows = cut(B, 2 * HD)
        v4 = cut(B, 2 * HD)
        kS = cut(2 * B, P + L)
        pS = cut(4, P + L)
        pTs = cut(4, P)
        pT4 = cut(4, P)
        oT = cut(SH, TS)
        aS = cut(4, 8)
        attn_end = top[0]
        top[0] = KC * T
        xr = cut(NT, D)
        xr_end = top[0]
        wo = cut(KC, D)
        wr = cut(KC, 72)
        nffn = cut(D)
        h2r = cut(2, D)
        h2T = cut(2, KC, P)
        brb = cut(72)
        lg = cut(NT, 72)
        rt = cut(NT, 64 * 6)
        g8v = cut(NT, 8)
        gnum = cut(NT, 8)
        el8 = cut(NT, 8)
        enum_ = cut(NT, 8)
        M = cut(NT, 3, 64)
        e64 = cut(8, 64)
        i16 = cut(16, 64)
        rsc = cut(NT, 16)
        m_lt = cut(P)
        wgu_at = 37632 - 2 * KC * 2 * FE
        assert top[0] <= wgu_at and attn_end <= wgu_at
        top[0] = 0
        X = cut(2, D)
        xT = cut(2, KC, P)
        hb = cut(2, FE)
        hid = cut(2, FE)
        hidT = cut(2, FE // P, P)
        ys = cut(2, D)
        assert top[0] <= xr_end
        top[0] = xr_end
        wgu1 = cut(2, KC, 2 * FE)
        wdn = (cut(2, FE // P, D), cut(2, FE // P, D))
        assert top[0] <= wgu_at
        top[0] = wgu_at
        wgu = (cut(2, KC, 2 * FE), wgu1)
        top[0] = 0
        yg = cut(2, 2, D)
        nfin = cut(D)
        yo = cut(2, D)
        ysq = cut(D)
        tokid = sb("tokid", [P, NT], I32)
        dsti = sb("dsti", [P, NT, 2], I32)
        wts = sb("wts", [P, NT, 2])
        ovt = sb("ovt", [1, 32], I32)
        sidx = sb("sidx", [P, NBLK // 2], I32)
        sidx2 = sb("sidx2", [P, 2], I32)
        ltab = co.rearrange("p a b -> p (a b)")[0:34, 0:1024].rearrange("p (v l r) -> p v l r", v=2, l=L)
        x2 = mixed
        hst = [Sb[:, :, :].rearrange("p a b -> p (a b)"), sm[:, :, :, :].rearrange("p a b c -> p (a b c)")]
        junk = gates.rearrange("p a b c -> p (a b c)")[:, 0:D]
        wbk = wrow.rearrange("p c g k -> p c (g k)")[:, :, 0:2 * H + 4 * HD]
        wkd = wch.rearrange("p c g k -> p c (g k)")[:, :, 0:4 * HD].rearrange("p c (v u d) -> p c v u d", v=2, u=2)
        ba = sc[:, 80:160].rearrange("p (n k) -> p n k", n=NT)
        alog = sc[:, 160:168]
        dtb = sc[:, 168:176]
        tmp = ex.rearrange("p a b -> p (a b)")
        relm = tmp[0:34, 1000:1385]
        rtab = tmp[0:34, 1385:1401]
        relr = tmp[0:SH, 600:984]

        s_setup = sem("setup")
        s_setup0 = sem("setup0")
        s_x_in = sem("x_in")
        s_wkd_in = sem("wkd_in")
        s_small_in = sem("small_in")
        s_rel_in = sem("rel_in")
        s_rel_out = sem("rel_out")
        s_bias_in = sem("bias_in")
        s_h_ready = sem("h_ready")
        s_hT_ps = sem("hT_ps")
        s_hT_ready = sem("hT_ready")
        s_kd_ps = sem("kd_ps")
        s_kd_done = sem("kd_done")
        s_bk_ps = sem("bk_ps")
        s_bk_done = sem("bk_done")
        s_ba_ready = sem("ba_ready")
        s_g_ready = sem("g_ready")
        s_g_ps = sem("g_ps")
        s_act_own = sem("act_own")
        s_dve_own = sem("dve_own")
        s_pool_own = sem("pool_own")
        s_rel_ps = sem("rel_ps")
        s_rel_done = sem("rel_done")
        s_wch_in = sem("wch_in")
        s_wrow_in = sem("wrow_in")
        s_cs_in = sem("cs_in")
        s_st_in = sem("st_in")
        s_proj_ps = sem("proj_ps")
        s_projs_ps = sem("projs_ps")
        s_cst_ps = sem("cst_ps")
        s_cst_ready = sem("cst_ready")
        s_raw_done = sem("raw_done")
        s_rows_ps = sem("rows_ps")
        s_rows_exp = sem("rows_exp")
        s_rows_done = sem("rows_done")
        s_ct_ready = sem("ct_ready")
        s_ct_ps = sem("ct_ps")
        s_crow_ready = sem("crow_ready")
        s_conv_done = sem("conv_done")
        s_exp_co = sem("exp_co")
        s_co_done = sem("co_done")
        s_sq_done = sem("sq_done")
        s_nrm_ps = sem("nrm_ps")
        s_rn_done = sem("rn_done")
        s_qk_done = sem("qk_done")
        s_lt_done = sem("lt_done")
        s_bS_done = sem("bS_done")
        s_y2_ps = sem("y2_ps")
        s_x2_done = sem("x2_done")
        s_h2_ready = sem("h2_ready")
        s_h2_out = sem("h2_out")
        s_h2T_ps = sem("h2T_ps")
        s_h2T_done = sem("h2T_done")
        s_lg_ps = sem("lg_ps")
        s_lg_done = sem("lg_done")
        s_mlt_done = sem("mlt_done")
        s_g_max = sem("g_max")
        s_g_exp = sem("g_exp")
        s_r_exp = sem("r_exp")
        s_e_dif = sem("e_dif")
        s_M_done = sem("M_done")
        s_rk_ps = sem("rk_ps")
        s_tok_done = sem("tok_done")
        s_slots_moved = sem("slots_moved")
        s_scat_out = sem("scat_out")
        s_route_done = sem("route_done")
        s_zi_done = sem("zi_done")
        s_ov_done = sem("ov_done")
        s_gu_in0 = sem("gu_in0")
        s_gu_in1 = sem("gu_in1")
        s_dn_in0 = sem("dn_in0")
        s_dn_in1 = sem("dn_in1")
        s_X_in0 = sem("X_in0")
        s_X_in1 = sem("X_in1")
        s_xt_ps = sem("xt_ps")
        s_xt_done = sem("xt_done")
        s_gu_ps = sem("gu_ps")
        s_hg_exp = sem("hg_exp")
        s_hid_done = sem("hid_done")
        s_hT2_ps = sem("hT2_ps")
        s_hT2_done = sem("hT2_done")
        s_dn_ps = sem("dn_ps")
        s_ye_a = sem("ye_a")
        s_ye_v = sem("ye_v")
        s_ye_out0 = sem("ye_out0")
        s_ye_out1 = sem("ye_out1")
        s_fin_in = sem("fin_in")
        s_yg_in0 = sem("yg_in0")
        s_yg_in1 = sem("yg_in1")
        s_yo_acc = sem("yo_acc")
        s_yo_fin = sem("yo_fin")
        s_yo_out = sem("yo_out")
        s_hid_own = sem("hid_own")
        s_stored = sem("stored")
        s_mT_act = sem("mT_act")
        s_rtab_set = sem("rtab_set")
        s_pe_passed = sem("pe_passed")
        s_pool_passed = sem("pool_passed")
        s_gm_ready = sem("gm_ready")
        s_D_ps = sem("D_ps")
        s_E_exp = sem("E_exp")
        s_Em_ready = sem("Em_ready")
        s_kk_ps = sem("kk_ps")
        s_kq_ps = sem("kq_ps")
        s_kr_ps = sem("kr_ps")
        s_vr_ps = sem("vr_ps")
        s_kvr_done = sem("kvr_done")
        s_Et_ps = sem("Et_ps")
        s_Et_done = sem("Et_done")
        s_attn_done = sem("attn_done")
        s_N_done = sem("N_done")
        s_Nt_ps = sem("Nt_ps")
        s_Nt_done = sem("Nt_done")
        s_Tt0_done = sem("Tt0_done")
        s_lev_p = sem("lev_p")
        s_lev_pt = sem("lev_pt")
        s_lev_t = sem("lev_t")
        s_ev_p = sem("ev_p")
        s_ev_pt = sem("ev_pt")
        s_ev_t = sem("ev_t")
        s_wT_ps = sem("wT_ps")
        s_wT_done = sem("wT_done")
        s_vn_ps = sem("vn_ps")
        s_vn_done = sem("vn_done")
        s_o_ps = sem("o_ps")
        s_sn_ps = sem("sn_ps")
        s_S_done = sem("S_done")
        s_o_done = sem("o_done")
        s_sE_exp = sem("sE_exp")
        s_sW_done = sem("sW_done")
        s_Vm_done = sem("Vm_done")
        s_sS_done = sem("sS_done")
        s_hs_ready = sem("hs_ready")
        s_decay_done = sem("decay_done")
        s_sc_ps = sem("sc_ps")
        s_sc_add = sem("sc_add")
        s_p_exp = sem("p_exp")
        s_pt_ps = sem("pt_ps")
        s_pt_done = sem("pt_done")
        s_pv_ps = sem("pv_ps")
        s_gate_done = sem("gate_done")
        s_ss_done = sem("ss_done")
        s_rstd_done = sem("rstd_done")
        s_mix_done = sem("mix_done")
        s_pdn_out = sem("pdn_out")
        s_sdn_out = sem("sdn_out")
        s_conv_out = sem("conv_out")
        s_kv_out = sem("kv_out")
        s_smp_ps = sem("smp_ps")
        s_smp_done = sem("smp_done")
        s_tail_in = sem("tail_in")
        s_cache_in = sem("cache_in")
        s_keys_in = sem("keys_in")
        s_att_dve = sem("att_dve")
        s_att_act = sem("att_act")
        s_att_ps = sem("att_ps")
        s_idx_ready = sem("idx_ready")
        gu_in, dn_in, X_in = (s_gu_in0, s_gu_in1), (s_dn_in0, s_dn_in1), (s_X_in0, s_X_in1)
        ye_out, yg_in = (s_ye_out0, s_ye_out1), (s_yg_in0, s_yg_in1)
        block = ctx.enter_context(nc.Block())

        def first_blocks(eng, pair):
            with eng.Fori(0, NPAIR // 2) as it:
                for a in range(2):
                    pair(it, a, None)

        def further_blocks(eng, pair):
            eng.wait_ge(s_ov_done, 1)
            more = eng.value_load(ovt[0:1, OV:OV + 1], min_val=0, max_val=OV)
            with eng.Fori(0, OV // 4) as it:
                with eng.If(it * 4 < more):
                    for a in range(2):
                        pair(it + NPAIR // 2, a, it)
            return more

        def later(it, a, k):
            return it + (a + k) // 2, (a + k) % 2
        gu_bank = (PB[2], PB[6])
        rows_of = [P] * NP + [TS]
        LV = 6

        @block.sync
        def _(sp):
            sp.dma_start(mixed[:, 0:NP, :], x_prompt.rearrange("(n p) d -> p n d", p=P)).then_inc(s_x_in, 16)
            sp.dma_start(mixed[0:TS, NP, :], x_sample).then_inc(s_x_in, 16)
            sp.dma_start(nmix, norm_mix_w.rearrange("(p c) -> p c", c=KC)).then_inc(s_x_in, 16)
            w_r = w_in.rearrange("(p c) k -> p c k", c=KC)
            for u in range(2):
                for v in range(2):
                    sp.dma_start(wkd[:, :, v, u, :], w_r[:, :, C_SK + v * HD:C_SK + (v + 1) * HD]).then_inc(s_wkd_in, 16)
            sp.dma_start(wbk[:, :, 0:2 * H], w_r[:, :, C_BA:C_BA + 2 * H]).then_inc(s_wkd_in, 16)
            sp.dma_start(wbk[:, :, 2 * H:], w_r[:, :, C_SK:C_SK + 4 * HD]).then_inc(s_wkd_in, 16)
            sp.dma_start(alog, a_log.partition_broadcast(P)).then_inc(s_small_in, 16)
            sp.dma_start(dtb, dt_bias.partition_broadcast(P)).then_inc(s_small_in, 16)
            sp.dma_start(dnw, dn_norm_w.partition_broadcast(P)).then_inc(s_small_in, 16)
            sp.dma_start(sinkb, sinks.partition_broadcast(P)).then_inc(s_small_in, 16)
            sp.dma_start(relm, rel_map).then_inc(s_rel_in, 16)
            sp.dma_start(rtab[0:32, :], rel_bias).then_inc(s_rel_in, 16)
            sp.dma_start(rtab[33:34, :], sinks.unsqueeze(0)).then_inc(s_rel_in, 16)
            sp.wait_ge(s_rel_done, 1)
            sp.dma_start(rel_d, relr.unsqueeze(1).to_broadcast([SH, P, 384])).then_inc(s_rel_out, 16)
            sp.wait_ge(s_rel_out, 16)
            sp.dma_start(bias, bass.AP(rel_d.tensor, 127, [[383, P], [P * 384, SH], [1, 256]])).then_inc(s_bias_in, 16)
            for k in range(2):
                sp.dma_start(ye_rows[:, NPAIR + k * NP:NPAIR + (k + 1) * NP, :], mixed[:, 0:NP, :]).then_inc(s_bias_in, 16)
            sp.wait_ge(s_kd_ps, 2)
            sp.wait_ge(s_bk_ps, NT)
            with sp.Fori(0, H) as h:
                sp.wait_ge(s_proj_ps, 1 + h * 4)
                for g, c0 in enumerate((0, GATE_W, 2 * GATE_W, C_SQ)):
                    sp.dma_start(wch[:, :, g, :], w_r[:, :, ds(h * P + c0, P)]).then_inc(s_wch_in, 16)
                sp.wait_ge(s_cst_ps, 1 + h)
                st_r = conv_state.rearrange("b s (g k) -> (b s) g k", g=3)
                cw_r = conv_w.rearrange("s (g k) -> s g k", g=3)
                sp.dma_start(cs[0:24, :, :], st_r[:, :, ds(h * P, P)]).then_inc(s_cs_in, 16)
                sp.dma_start(cs[24:28, :, :], cw_r[:, :, ds(h * P, P)]).then_inc(s_cs_in, 16)
                sp.wait_ge(s_rows_ps, 1 + h * NT)
                for g, c0 in enumerate((C_Z, C_GA, C_GB)):
                    sp.dma_start(wrow[:, :, g, :], w_r[:, :, ds(h * P + c0, P)]).then_inc(s_wrow_in, 16)
                sp.wait_ge(s_stored, 1 + h)
                sp.dma_start(Sb[:, :, :], dn_state.rearrange("b h k v -> h k b v")[ds(h), :, :, :].rearrange("a k b v -> (a k) b v")).then_inc(s_st_in, 16)

            ck = cache_k.rearrange("b s (v d) -> s b v d", v=2)
            sp.wait_ge(s_cst_ps, 1 + H)
            sp.wait_ge(s_conv_done, 3 * H)
            sp.wait_ge(s_ct_ready, H)
            for u in range(2):
                for v in range(2):
                    sp.dma_start(krows[:, :, v, u, :], ck[:, :, v, :]).then_inc(s_keys_in, 16)
            sp.wait_ge(s_qk_done, H)
            sp.wait_ge(s_vr_ps, H)
            sp.wait_ge(s_smp_ps, 11 * (H - 1) + 1)
            sp.dma_start(vrows, cache_v.rearrange("b s k -> s b k")).then_inc(s_cache_in, 16)
            sp.wait_ge(s_keys_in, 64)
            sp.wait_ge(s_rows_ps, 1 + H * NT)
            sp.wait_ge(s_sc_add, H * NP)
            sp.dma_start(wo, w_out.rearrange("(p c) k -> p c k", c=KC)).then_inc(s_keys_in, 16)
            sp.wait_ge(s_mix_done, 1 + H * NT)
            sp.wait_ge(s_stored, 1 + H)
            sp.wait_ge(s_sS_done, 1 + H)
            for b in range(B):
                sp.dma_start(v4[0:L, b, :], kvrow[b * L:(b + 1) * L, NP, 2 * HD:]).then_inc(s_cache_in, 16)

            def load_gate_up(a, k, e):
                sp.dma_start(wgu[a][:, k, :, 0:FE], w_gate[ds(e), :, :].rearrange("a (p c) f -> p (a c) f", c=KC)).then_inc(gu_in[a], 16)
                sp.dma_start(wgu[a][:, k, :, FE:], w_up[ds(e), :, :].rearrange("a (p c) f -> p (a c) f", c=KC)).then_inc(gu_in[a], 16)

            def load_down(a, k, e):
                sp.dma_start(wdn[a][:, k, :, :], w_down[ds(e), :, :].rearrange("a (p c) k -> p (a c) k", c=FE // P)).then_inc(dn_in[a], 16)

            load_gate_up(0, 0, 0)
            sp.wait_ge(s_att_ps, 8)
            sp.dma_start(xr[:, 0:NP, :], x_prompt.rearrange("(n p) d -> p n d", p=P)).then_inc(s_tail_in, 16)
            sp.dma_start(xr[0:TS, NP, :], x_sample).then_inc(s_tail_in, 16)
            sp.dma_start(wr[:, :, 0:8], w_rg.rearrange("(p c) k -> p c k", c=KC)).then_inc(s_tail_in, 16)
            sp.dma_start(wr[:, :, 8:72], w_re.rearrange("(p c) k -> p c k", c=KC)).then_inc(s_tail_in, 16)
            sp.dma_start(nffn, norm_ffn_w.partition_broadcast(P)).then_inc(s_tail_in, 16)
            sp.dma_start(brb[:, 0:8], b_rg.partition_broadcast(P)).then_inc(s_tail_in, 16)
            sp.dma_start(brb[:, 8:72], b_re.partition_broadcast(P)).then_inc(s_tail_in, 16)
            load_gate_up(0, 1, 1)
            for n in range(NT):
                sp.wait_ge(s_h2_ready, n + 1)
                sp.dma_start(h2_d[n * P:n * P + rows_of[n], :], h2r[0:rows_of[n], n % 2, :]).then_inc(s_h2_out, 16)
                sp.wait_ge(s_h2_out, 16 * (n + 1))
            sp.wait_ge(s_y2_ps, NT)
            for k in range(2):
                load_gate_up(1, k, 2 + k)
            sp.wait_ge(s_lg_ps, NT)
            for k in range(2):
                load_down(0, k, k)
            sp.wait_ge(s_route_done, 1)

            def gate_up_weights(it, a):
                sp.wait_ge(s_gu_ps, 1 + it * 2 + a)
                for k in range(2):
                    load_gate_up(a, k, it * 4 + (2 * a + k))

            def down_weights(it, a):
                sp.wait_ge(s_dn_ps, 1 + it * 2 + a)
                for k in range(2):
                    load_down(a, k, it * 4 + (2 * a + k))

            with sp.Fori(1, NPAIR // 2) as it:
                gate_up_weights(it, 0)
                down_weights(it - 1, 1)
                gate_up_weights(it, 1)
                down_weights(it, 0)
            down_weights(NPAIR // 2 - 1, 1)

            def load(it, a, more):
                sp.wait_ge(s_gu_ps, 1 + it * 2 + a)
                sp.wait_ge(s_dn_ps, 1 + it * 2 + a)
                for k in range(2):
                    e = sp.value_load(ovt[0:1, ds(more * 4 + (2 * a + k))], min_val=0, max_val=NE - 1)
                    load_gate_up(a, k, e)
                    load_down(a, k, e)

            further_blocks(sp, load)
            sp.wait_ge(s_tok_done, 1)
            sp.dma_start(nfin, norm_final_w.partition_broadcast(P)).then_inc(s_fin_in, 16)
            for n in range(NT):
                R = rows_of[n]
                sp.wait_ge(s_yo_fin, n + 1)
                dst = y_p[n * P:(n + 1) * P, :] if n < NP else y_s
                sp.dma_start(dst, yo[0:R, n % 2, :]).then_inc(s_yo_out, 16)
                sp.wait_ge(s_yo_out, 16 * (n + 1))

        @block.gpsimd
        def _(pool):
            ch = Chain(pool, s_pool_own)
            step = ch.step
            for s in (s_proj_ps, s_projs_ps, s_cst_ps, s_rows_ps, s_mix_done, s_gate_done, s_o_done, s_sS_done, s_rows_done, s_stored, s_xt_done, s_ye_a, s_ye_v, *ye_out):
                pool.sem_inc(s, 1)
            pool.sem_inc(s_gu_ps, 2)
            pool.sem_inc(s_dn_ps, 2)
            pool.sem_inc(s_xt_ps, 3)
            for t in (ones[:, :], m_le[:, :], m_gt[:, :], m_ge[:, :], blk[:, :, :], bsel[:, :]):
                ch.inc(pool.memset(t, 1.0))
            ch.inc(pool.memset(ident[:, :], 0.0))
            for t in (rawP[:, :, 0:3], kz, qz.rearrange("p b v u k -> p (b v u k)"), scal, sc[:, 80:160]):
                ch.inc(pool.memset(t, 0.0))
            pool.memset(eps_t[:, 0:1], EPS).then_inc(s_setup0, 1)
            pool.memset(eps_t[:, 1:2], -0.5 * 4.852030263919617).then_inc(s_setup0, 1)
            pool.wait_ge(s_pool_own, ch.value())

            def keep(t, base, pat, mult, op=ALU.is_ge, fill=0.0):
                return pool.affine_select(out=t, in_=t, compare_op=op, fill=fill, base=base, pattern=pat,
                                          channel_multiplier=mult)

            ch.inc(keep(ident[:, :], 0, [[-1, P]], 1, ALU.not_equal, 1.0))
            ch.inc(keep(m_le[:, :], 0, [[1, P]], -1))
            ch.inc(keep(m_gt[:, :], -1, [[-1, P]], 1))
            ch.inc(keep(m_ge[:, :], 0, [[-1, P]], 1))
            ch.inc(keep(blk[:, :, :], 0, [[-L, B], [0, L]], 1))
            step(keep(bsel[:, :], 0, [[-L, B]], 1))
            ch.inc(keep(blk[:, :, :], L - 1, [[L, B], [0, L]], -1))
            step(keep(bsel[:, :], L - 1, [[L, B]], -1))
            bf = blk[:, :, :].rearrange("p b l -> p (b l)")
            pool.tensor_tensor(s_le[:, :], bf, m_le[0:TS, 0:TS], ALU.mult).then_inc(s_setup, 1)
            pool.tensor_tensor(s_gt[:, :], bf, m_gt[0:TS, 0:TS], ALU.mult).then_inc(s_setup, 1)
            pool.tensor_tensor(s_ge[:, :], bf, m_ge[0:TS, 0:TS], ALU.mult).then_inc(s_setup, 1)
            pool.iota(tokid[:, :], pattern=[[P, NT]], base=0, channel_multiplier=1).then_inc(s_zi_done, 1)
            zi = wqo[:, :, :].rearrange("p a b -> p (a b)")[:, 0:NS // P].bitcast(I32)
            pool.memset(zi, 0).then_inc(s_zi_done, 1)
            pool.memset(ltab, 0.0).then_inc(s_zi_done, 1)
            pool.wait_ge(s_zi_done, 2)
            pool.dma_start(slot_d.rearrange("(p c) k -> p (c k)", p=P), zi).then_inc(s_slots_moved, 16)
            pool.wait_ge(s_setup, 3)
            W = cache_k.shape[1]
            pool.dma_start(s_k[:, 0:W - L, :], cache_k[:, L:W, :]).then_inc(s_kv_out, 16)
            pool.dma_start(s_v[:, 0:W - L, :], cache_v[:, L:W, :]).then_inc(s_kv_out, 16)
            pool.wait_ge(s_bk_done, NT)
            pool.dma_start(p_k, kvrow[:, NP - 1, 0:2 * HD]).then_inc(s_kv_out, 16)
            pool.dma_start(p_v, kvrow[:, NP - 1, 2 * HD:]).then_inc(s_kv_out, 16)
            for b in range(B):
                pool.dma_start(s_k[b, W - L:W, :], kvrow[b * L:(b + 1) * L, NP, 0:2 * HD]).then_inc(s_kv_out, 16)
                pool.dma_start(s_v[b, W - L:W, :], kvrow[b * L:(b + 1) * L, NP, 2 * HD:]).then_inc(s_kv_out, 16)
            pool.wait_ge(s_small_in, 64)
            with pool.Fori(0, H) as h:
                pool.wait_ge(s_hs_ready, h * 2 + 1)
                pool.tensor_tensor(gm, m_le[:, :].unsqueeze(1).to_broadcast([P, NP, P]),
                                   hsc[:, 0, 0:NP].unsqueeze(2).to_broadcast([P, NP, P]), ALU.mult).then_inc(s_gm_ready, 1)
                pool.tensor_scalar(sS[:, 8, 0:TS], s_le[:, :], hsc[0:TS, 0, NP:NT], None, ALU.mult).then_inc(s_gm_ready, 1)
                pool.wait_ge(s_E_exp, h + 1)
                pool.tensor_tensor(Es, E, m_gt[:, :].unsqueeze(1).to_broadcast([P, NP, P]), ALU.mult).then_inc(s_Em_ready, 1)
                pool.wait_ge(s_Em_ready, h * 2 + 1)
                pool.tensor_tensor(E, E, m_ge[:, :].unsqueeze(1).to_broadcast([P, NP, P]), ALU.mult).then_inc(s_Em_ready, 1)
                for n in range(NT):
                    R = rows_of[n]
                    pool.wait_ge(s_rows_done, 1 + h * NT + (n + 1))
                    pool.tensor_tensor(gates[0:R, n, 0, :], gates[0:R, n, 0, :], gates[0:R, n, 1, :], ALU.mult).then_inc(s_ss_done, 1)
                    pool.wait_ge(s_ss_done, h * NT + (n + 1))
                    pool.tensor_tensor(gates[0:R, n, 0, :], gates[0:R, n, 0, :], dnw[0:R, :], ALU.mult).then_inc(s_gate_done, 1)
                    if n == 1:
                        pool.wait_ge(s_crow_ready, h + 1)
                        pool.sem_inc(s_pool_passed, 1)
                        pool.dma_start(p_conv[:, :, ds(h * P, P)], crow[0:3, :, :]).then_inc(s_conv_out, 16)
                        pool.dma_start(s_conv[:, :, ds(h * P, P)], crow[3:27, :, :]).then_inc(s_conv_out, 16)
                pool.wait_ge(s_smp_ps, h * 11 + 8)
                pool.tensor_tensor(Sb[:, :, :], Sb[:, :, :], hgl.unsqueeze(2).to_broadcast([P, B, P]), ALU.mult).then_inc(s_decay_done, 1)
                pool.wait_ge(s_sW_done, h * 3 + 3)
                pool.tensor_tensor(Vm[:, :, :], sS[:, 6, :].unsqueeze(1).to_broadcast([TS, B, P]),
                                   bsel[:, :].unsqueeze(2).to_broadcast([TS, B, P]), ALU.mult).then_inc(s_Vm_done, 1)
                pool.wait_ge(s_S_done, h * NP + NP)
                pool.sem_inc(s_pool_passed, 1)
                pool.dma_start(p_dn[ds(h), :, :].rearrange("a k v -> (a k) v"), St).then_inc(s_pdn_out, 16)
                pool.wait_ge(s_sS_done, 1 + h + 1)
                pool.sem_inc(s_pool_passed, 1)
                pool.dma_start(s_dn.rearrange("b h k v -> h k b v")[ds(h), :, :, :].rearrange("a k b v -> (a k) b v"), Sb[:, :, :]).then_inc(s_sdn_out, 16)
                pool.wait_ge(s_conv_out, h * 32 + 32)
                pool.wait_ge(s_pdn_out, h * 16 + 16)
                pool.wait_ge(s_sdn_out, h * 16 + 16)
                pool.sem_inc(s_stored, 1)
            pool.wait_ge(s_pdn_out, 16 * H)
            pool.wait_ge(s_sdn_out, 16 * H)
            pool.wait_ge(s_conv_out, 32 * H)
            pool.wait_ge(s_kv_out, 16 * (4 + 2 * B))
            pool.wait_ge(s_att_ps, 8)
            ch.inc(pool.iota(e64[:, 0, :], pattern=[[1, 64]], base=0, channel_multiplier=0, allow_small_or_imprecise_dtypes=True))
            ch.inc(pool.iota(i16[:, :, :], pattern=[[1, 16], [0, 64]], base=0, channel_multiplier=0, allow_small_or_imprecise_dtypes=True))
            pool.wait_ge(s_pool_own, ch.value())
            pool.tensor_tensor(m_lt, ones[:, :], m_ge[:, :], ALU.subtract).then_inc(s_mlt_done, 1)
            pool.wait_ge(s_M_done, 1)
            pool.wait_ge(s_slots_moved, 16)
            for n in range(NT):
                R = rows_of[n]
                for k in range(2):
                    pool.indirect_dma_start(slot_d[:, :], bass.IndirectOffsetOnAxis(ap=dsti[0:R, n, k:k + 1], axis=0),
                                            tokid[0:R, n:n + 1], None).then_inc(s_scat_out, 16)
            pool.wait_ge(s_scat_out, 16 * 2 * NT)
            pool.wait_ge(s_h2_out, 16 * NT)

            pool.dma_start(sidx[:, :], slot_d.rearrange("(p j) k -> p (j k)", p=P)).then_inc(s_slots_moved, 16)
            pool.wait_ge(s_slots_moved, 32)

            def gather(it, a, more):
                j = it * 2 + a
                pool.wait_ge(s_xt_ps, 1 + j * 2)
                pool.tensor_copy(sidx2[:, a:a + 1], sidx[:, ds(j)]).then_inc(s_idx_ready, 1)
                pool.wait_ge(s_idx_ready, j + 1)
                pool.sem_inc(s_pool_passed, 1)
                pool.indirect_dma_start(X[:, a, :], None, h2_d[:, :], bass.IndirectOffsetOnAxis(ap=sidx2[:, a:a + 1], axis=0)).then_inc(X_in[a], 16)

            first_blocks(pool, gather)
            further_blocks(pool, gather)
            pool.wait_ge(s_tok_done, 1)
            for n in range(NT):
                R = rows_of[n]
                if n >= 2:
                    pool.wait_ge(s_yo_acc, n - 1)
                for k in range(2):
                    pool.indirect_dma_start(yg[0:R, n % 2, k, :], None, ye_d[:, :], bass.IndirectOffsetOnAxis(ap=dsti[0:R, n, k:k + 1], axis=0)).then_inc(yg_in[n % 2], 16)

        @block.scalar
        def _(act):
            ch = Chain(act, s_act_own)
            step = ch.step
            nc.add_instruction(mybir.InstLoadActFuncSet(act_func_set_id=LN_EXP_SET, name=nc.get_next_instruction_name(), engine=mybir.EngineType.Activation))
            act.wait_ge(s_setup0, 2)
            act.wait_ge(s_x_in, 48)
            for n in range(NT):
                R = rows_of[n]
                step(act.activation(junk[0:R, :], mixed[0:R, n, :], ACT.Square, accum_out=sc[0:R, n:n + 1]))
                step(act.activation(sc[0:R, 8 + n:9 + n], sc[0:R, n:n + 1], ACT.Ln, scale=1.0 / D, bias=eps_t[0:R, 0:1]))
                step(act.activation(sc[0:R, 16 + n:17 + n], sc[0:R, 8 + n:9 + n], ACT.Exp, scale=-0.5))
                if n >= 2:
                    act.wait_ge(s_hT_ps, 2 * (n - 1))
                act.activation(hst[n % 2][0:R, :], mixed[0:R, n, :], ACT.Copy, scale=sc[0:R, 16 + n:17 + n]).then_inc(s_h_ready, 1)
            act.wait_ge(s_rel_ps, 1)
            act.activation(relr, PB[7][0:SH, 0:384], ACT.Copy).then_inc(s_rel_done, 1)
            g8 = lambda k: tmp[:, 40 * k:40 * k + 40].rearrange("p (n h) -> p n h", n=NT)
            act.wait_ge(s_small_in, 64)
            act.wait_ge(s_ba_ready, 1)
            act.activation(g8(0), ba[:, :, 0:H], ACT.Exp, scale=-1.0).then_inc(s_g_ready, 1)
            act.activation(g8(2), g8(1), ACT.Exp, scale=-1.0).then_inc(s_g_ready, 1)
            act.activation(tmp[:, 160:168], alog, ACT.Exp).then_inc(s_g_ready, 1)
            act.wait_ge(s_ba_ready, 2)
            act.activation(g8(2), g8(2), ACT.Ln).then_inc(s_g_ready, 1)
            for v in range(2):
                act.wait_ge(s_kd_ps, v + 1)
                act.activation(kz[0:HD, 0, v, :], PB[4 + v][0:HD, :], ACT.Copy).then_inc(s_kd_done, 1)
                act.activation(kz[HD:P, 1, v, :], PB[4 + v][HD:P, :], ACT.Copy).then_inc(s_kd_done, 1)
                act.activation(skd[:, v, :], PB[2 + v][:, 0:TS], ACT.Copy).then_inc(s_kd_done, 1)
            act.wait_ge(s_ba_ready, 6)
            gs = tmp[:, 280:424]
            act.activation(scal[:, 3, 0:NP, :], gs[:, 0:32].rearrange("p (n h) -> p n h", n=NP), ACT.Exp).then_inc(s_g_ready, 1)
            act.activation(scal[:, 5, 0:NP, :], gs[:, 32:64].rearrange("p (n h) -> p n h", n=NP), ACT.Exp).then_inc(s_g_ready, 1)
            act.activation(scal[0:TS, 3, NP, :], gs[0:TS, 64:72], ACT.Exp).then_inc(s_g_ready, 1)
            act.activation(glS, gs[:, 80:144].rearrange("p (b h) -> p b h", b=B), ACT.Exp).then_inc(s_g_ready, 1)
            act.wait_ge(s_ba_ready, 7)
            act.activation(scal[:, 4, 0:NP, :], tmp[:, 200:232].rearrange("p (n h) -> p n h", n=NP), ACT.Exp).then_inc(s_g_ready, 1)
            act.activation(scal[0:TS, 4, NP, :], tmp[0:TS, 232:240], ACT.Exp).then_inc(s_g_ready, 1)

            KCH = 3 + NT + 2
            with act.Fori(0, H) as h:
                ch.loop(h, KCH)
                act.wait_ge(s_cst_ps, 1 + h + 1)
                act.activation(cst, PB[7][:, 0:84].rearrange("p (g k) -> p g k", g=3), ACT.Copy).then_inc(s_cst_ready, 1)
                kv, hh = h // 4, h % 4
                for g in range(4):
                    act.wait_ge(s_proj_ps, 1 + h * 4 + (g + 1))
                    if g < 3:
                        act.activation(rawP[:, g, 3:], PB[g][:, :], ACT.Copy).then_inc(s_raw_done, 1)
                    else:
                        act.activation(sqT, PB[g][:, :], ACT.Copy, scale=HD ** -0.5).then_inc(s_raw_done, 1)
                    if g == 0:
                        act.wait_ge(s_projs_ps, 1 + h + 1)
                        act.activation(rawS[:, :, :, 3:], PB[4][:, 0:96].rearrange("p (g b l) -> p g b l", g=3, b=B), ACT.Copy).then_inc(s_raw_done, 1)
                        for u in range(2):
                            act.activation(qz[u * HD:(u + 1) * HD, :, ds(kv), u, ds(hh * L, L)].rearrange("p b a l -> p b (a l)"),
                                           PB[4][u * HD:(u + 1) * HD, 96:128].rearrange("p (b l) -> p b l", b=B),
                                           ACT.Copy, scale=HD ** -0.5).then_inc(s_raw_done, 1)
                    if g < 3:
                        act.wait_ge(s_conv_done, h * 3 + (g + 1))
                        act.activation(ex[:, g, :], co[:, g, :], ACT.Exp, scale=-1.0).then_inc(s_exp_co, 1)
                act.wait_ge(s_co_done, h * 3 + 2)
                act.activation(ex[:, 0:2, :], co[:, 0:2, :], ACT.Square).then_inc(s_sq_done, 1)
                def gate_exp(n):
                    R = rows_of[n]
                    act.wait_ge(s_rows_ps, 1 + h * NT + (n + 1))
                    if n >= 2:
                        act.wait_ge(s_rows_done, 1 + h * NT + (n - 1))
                    act.activation(sig[0:R, n % 2, :, :], PB[5 + n % 2][0:R, 0:3 * P].rearrange("p (g k) -> p g k", g=3), ACT.Exp, scale=-1.0).then_inc(s_rows_exp, 1)

                gate_exp(0)
                act.wait_ge(s_D_ps, h + 1)
                act.activation(E, PB[7][:, :].rearrange("p (n k) -> p n k", n=NP), ACT.Exp).then_inc(s_E_exp, 1)
                gate_exp(1)
                act.wait_ge(s_ct_ps, h + 1)
                act.wait_ge(s_stored, 1 + h)
                act.activation(crow[0:27, :, :], PB[4][0:27, 128:512].rearrange("p (g k) -> p g k", g=3), ACT.Copy).then_inc(s_crow_ready, 1)
                act.wait_ge(s_nrm_ps, h + 1)
                for g in range(2):
                    ch.inc(act.activation(qk[:, g, 0:TP], PB[g][:, :], ACT.Ln, bias=eps_t[:, 0:1]))
                step(act.activation(qk[:, :, TP:T], PB[4][:, 0:64].rearrange("p (g k) -> p g k", g=2), ACT.Ln, bias=eps_t[:, 0:1]))
                act.activation(qk[:, 0, :], qk[:, 0, :], ACT.Exp, scale=-0.5, bias=eps_t[:, 1:2]).then_inc(s_rn_done, 1)
                act.activation(qk[:, 1, :], qk[:, 1, :], ACT.Exp, scale=-0.5).then_inc(s_rn_done, 1)
                gate_exp(2)
                act.wait_ge(s_Et_ps, h + 1)
                act.activation(Et, PB[7][:, :].rearrange("p (n k) -> p n k", n=NP), ACT.Copy).then_inc(s_Et_done, 1)
                gate_exp(3)
                act.wait_ge(s_Nt_ps, h + 1)
                act.activation(PT[:, 0, :, :], PB[3][:, :].rearrange("p (n k) -> p n k", n=NP), ACT.Copy).then_inc(s_Nt_done, 1)

                def power(k):
                    act.wait_ge(s_lev_p, h * LV + k)
                    act.activation(PW[:, k % 2, :, :], PB[0][:, :].rearrange("p (n k) -> p n k", n=NP), ACT.Copy).then_inc(s_ev_p, 1)

                def probs(n):
                    lo = P if n == 0 else 0
                    a = att[:, n % 2, :]
                    act.wait_ge(s_sc_add, h * NP + (n + 1))
                    for u in range(2):
                        act.activation(sm[:, n % 2, u, lo:], sm[:, n % 2, u, lo:], ACT.Exp, bias=a[:, 2 + u:3 + u],
                                       accum_out=a[:, 6 + u:7 + u]).then_inc(s_p_exp, 1)
                    act.activation(esk[:, n % 2, :], a[:, 4:6], ACT.Exp).then_inc(s_p_exp, 1)

                def ptc(n):
                    act.wait_ge(s_pt_ps, h * NP + (n + 1))
                    if n > 0:
                        act.wait_ge(s_pv_ps, h * NP + n)
                    k = 2 if n == 0 else 4
                    act.activation(pT[:, 0:k, :], PB[3][:, 0:k * P].rearrange("p (a k) -> p a k", k=P), ACT.Copy).then_inc(s_pt_done, 1)

                power(1)
                gate_exp(4)
                act.wait_ge(s_smp_ps, h * 11 + 2)
                act.activation(sS[:, 3, 0:TS], PB[6][0:TS, 0:TS], ACT.Exp).then_inc(s_sE_exp, 1)
                power(2)
                probs(0)
                power(3)
                probs(1)
                ptc(0)
                power(4)
                probs(2)
                ptc(1)
                power(5)
                probs(3)
                ptc(2)
                power(6)
                ptc(3)
                act.wait_ge(s_smp_ps, h * 11 + 7)
                act.activation(wqT[:, :, 0, :], PB[6][:, 480:512].rearrange("p (b l) -> p b l", b=B), ACT.Copy, scale=-1.0).then_inc(s_sW_done, 1)
                act.activation(wqT[:, :, 1, :], qk[:, 0, TP:T].rearrange("p (b l) -> p b l", b=B), ACT.Copy).then_inc(s_sW_done, 1)
                act.wait_ge(s_wT_ps, h + 1)
                act.activation(nwT, PB[3][:, :].rearrange("p (n k) -> p n k", n=NP), ACT.Copy, scale=-1.0).then_inc(s_wT_done, 1)
                for n in range(NP):
                    act.wait_ge(s_vn_ps, h * NP + (n + 1))
                    act.activation(vnew[:, n, :], PB[0][:, n * P:(n + 1) * P], ACT.Copy).then_inc(s_vn_done, 1)
                    if n == 1:
                        act.wait_ge(s_smp_ps, h * 11 + 9)
                        act.activation(sS[:, 6, :], PB[6][0:TS, 64:192], ACT.Copy).then_inc(s_sW_done, 1)
                for n in range(NT):
                    R = rows_of[n]
                    act.wait_ge(s_o_done, 1 + h * NT + (n + 1))
                    ch.inc(act.activation(sig[0:R, n // 3, n % 3, :], orow[0:R, n, :], ACT.Square, accum_out=ssq[0:R, 0, n:n + 1]))
                act.wait_ge(s_act_own, ch.value())
                ch.inc(act.activation(ssq[:, 1, 0:NP], ssq[:, 0, 0:NP], ACT.Ln, scale=1.0 / P, bias=eps_t[:, 0:1]))
                step(act.activation(ssq[0:TS, 1, NP:NT], ssq[0:TS, 0, NP:NT], ACT.Ln, scale=1.0 / P, bias=eps_t[0:TS, 0:1]))
                act.activation(ssq[:, 2, 0:NP], ssq[:, 1, 0:NP], ACT.Exp, scale=-0.5).then_inc(s_rstd_done, 1)
                act.activation(ssq[0:TS, 2, NP:NT], ssq[0:TS, 1, NP:NT], ACT.Exp, scale=-0.5).then_inc(s_rstd_done, 1)
            ch.end(H)
            cpa = lambda o, i, **k: act.activation(o, i, ACT.Copy, **k)
            for k in range(4):
                act.wait_ge(s_att_ps, k + 1)
                cpa(kS[:, 4 * k:4 * k + 4, 0:P], PB[k][:, :].rearrange("p (a k) -> p a k", a=4)).then_inc(s_att_act, 1)
            act.wait_ge(s_att_dve, 2)
            for g in range(4):
                ch.inc(act.activation(pS[:, g, :], pS[:, g, :], ACT.Exp, bias=aS[:, g, 1:2], accum_out=aS[:, g, 3:4]))
            act.activation(aS[:, :, 4:5], aS[:, :, 2:3], ACT.Exp).then_inc(s_att_act, 1)
            act.wait_ge(s_act_own, ch.value())
            act.sem_inc(s_att_act, 1)
            act.wait_ge(s_att_ps, 6)
            cpa(pTs, PB[0][:, :].rearrange("p (a k) -> p a k", a=4)).then_inc(s_att_act, 1)
            cpa(pT4[0:L, :, :], PB[1][0:L, :].rearrange("p (a k) -> p a k", a=4)).then_inc(s_att_act, 1)
            act.wait_ge(s_att_ps, 7)
            for v in range(2):
                for u in range(2):
                    cpa(oT[0:HD, :, :].rearrange("p (v k u) (b l) -> p v u b k l", v=2, u=2, b=B)[:, v, u, :, :, :],
                        PB[2][0:HD, :].rearrange("p (b v u k l) -> p v u b k l", b=B, v=2, u=2, k=4)[:, v, u, :, :, :]).then_inc(s_att_act, 1)
            for n in range(NT):
                R = rows_of[n]
                act.wait_ge(s_hT_ps, 2 * NT + (2 * n + 1))
                cpa(hT[:, 0:4, n * P:n * P + R], PB[2 * (n % 2)][:, :].rearrange("p (c k) -> p c k", c=4)[:, :, 0:R]).then_inc(s_mT_act, 1)
            for n in range(NT):
                R = rows_of[n]
                act.wait_ge(s_x2_done, n + 1)
                step(act.activation(hst[0][0:R, :], x2[0:R, n, :], ACT.Square, accum_out=rsc[0:R, n, 0:1]))
                step(act.activation(rsc[0:R, n, 1:2], rsc[0:R, n, 0:1], ACT.Ln, scale=1.0 / D, bias=eps_t[0:R, 0:1]))
                act.activation(rsc[0:R, n, 2:3], rsc[0:R, n, 1:2], ACT.Exp, scale=-0.5).then_inc(s_r_exp, 1)
                act.wait_ge(s_h2T_ps, 2 * n + 1)
                if n >= 2:
                    act.wait_ge(s_lg_ps, n - 1)
                cpa(h2T[:, n % 2, 0:4, 0:R], PB[6][:, :].rearrange("p (c k) -> p c k", c=4)[:, :, 0:R]).then_inc(s_h2T_done, 1)
            for n in range(NT):
                R = rows_of[n]
                act.wait_ge(s_g_max, n + 1)
                ch.inc(act.activation(rt[0:R, n, 0:8], lg[0:R, n, 0:8], ACT.Exp, bias=rsc[0:R, n, 3:4], accum_out=rsc[0:R, n, 4:5]))
                act.activation(rsc[0:R, n, 6:7], rsc[0:R, n, 5:6], ACT.Exp).then_inc(s_g_exp, 1)
            act.wait_ge(s_act_own, ch.value())
            act.sem_inc(s_g_exp, 1)
            act.wait_ge(s_route_done, 1)

            def turned(it, a):
                j = it * 2 + a
                act.wait_ge(s_xt_ps, 3 + j * 2 + 1)
                cpa(xT[:, a, 0:4, :], PB[0][:, :].rearrange("p (c k) -> p c k", c=4)).then_inc(s_xt_done, 1)

            def exp_gate(it, a):
                j = it * 2 + a
                act.wait_ge(s_gu_ps, 2 + j + 1)
                act.activation(hb[:, a, :], gu_bank[a][:, 0:FE], ACT.Exp, scale=-1.0).then_inc(s_hg_exp, 1)

            def hid_turned(it, a):
                j = it * 2 + a
                act.wait_ge(s_hT2_ps, j + 1)
                cpa(hidT[:, a, :, :], PB[3][:, 0:FE].rearrange("p (c k) -> p c k", c=FE // P)).then_inc(s_hT2_done, 1)

            def rows_out(it, a):
                j = it * 2 + a
                act.wait_ge(s_dn_ps, 2 + j + 1)
                act.wait_ge(ye_out[a], 1 + it * 16)
                cpa(ys[:, a, 0:512], PB[4][:, :]).then_inc(s_ye_a, 1)
                act.wait_ge(s_ye_a, 1 + j + 1)
                act.wait_ge(s_ye_v, 1 + j + 1)
                act.dma_start(ye_rows[:, ds(j), :].rearrange("p j d -> p (j d)"), ys[:, a, :]).then_inc(ye_out[a], 16)

            def follow(it, a, nxt=True, turn=True):
                hid_turned(it, a)
                if nxt:
                    exp_gate(*later(it, a, 1))
                if turn:
                    turned(*later(it, a, 2))
                rows_out(it, a)

            turned(0, 0)
            exp_gate(0, 0)
            turned(0, 1)
            with act.Fori(0, NPAIR // 2 - 1) as it:
                for a in range(2):
                    follow(it, a)
            follow(NPAIR // 2 - 1, 0, turn=False)
            follow(NPAIR // 2 - 1, 1, nxt=False, turn=False)

            def further(it, a, k):
                turned(it, a)
                exp_gate(it, a)
                hid_turned(it, a)
                rows_out(it, a)

            more = further_blocks(act, further)
            turns = (more + 3) // 4
            for a in range(2):
                act.wait_ge(ye_out[a], 1 + turns * 16 + 16 * (NPAIR // 2))
            act.sem_inc(s_tok_done, 1)
            for n in range(NT):
                R = rows_of[n]
                act.wait_ge(s_yo_acc, n + 1)
                step(act.activation(ysq[0:R, :], x2[0:R, n, :], ACT.Square, accum_out=sc[0:R, n:n + 1]))
                step(act.activation(sc[0:R, 8 + n:9 + n], sc[0:R, n:n + 1], ACT.Ln, scale=1.0 / D, bias=eps_t[0:R, 0:1]))
                act.activation(sc[0:R, 16 + n:17 + n], sc[0:R, 8 + n:9 + n], ACT.Exp, scale=-0.5).then_inc(s_r_exp, 1)

        @block.tensor
        def _(pe):
            mm, tr = pe.matmul, pe.transpose
            pe.wait_ge(s_setup, 3)
            for n in range(NT):
                R = rows_of[n]
                pe.wait_ge(s_h_ready, n + 1)
                if n >= 2:
                    pe.wait_ge(s_hT_ready, 2 * (n - 1))
                for q in range(2):
                    for j in range(4):
                        last = tr(PB[2 * (n % 2) + q][:, j * P:j * P + R], hst[n % 2][0:R, 4 * q + j:D:KC], ident[0:R, 0:R])
                    last.then_inc(s_hT_ps, 1)
            pe.wait_ge(s_rel_in, 48)
            pe.wait_ge(s_rtab_set, 1)
            mm(PB[7][0:SH, 0:384], rtab, relm[:, 0:384], start=True, stop=True).then_inc(s_rel_ps, 1)
            pe.wait_ge(s_lt_done, 16)
            for v in range(2):
                for l in range(L):
                    mm(PB[5][:, v * 133:v * 133 + 132], ltab[:, v, l, :], relm[:, 127 - l:259 - l], start=l == 0, stop=l == L - 1)
                for l in range(L):
                    last = mm(PB[5][:, v * 133 + 132:v * 133 + 133], ltab[:, v, l, :], relm[:, 384:385], start=l == 0, stop=l == L - 1)
            last.then_inc(s_rel_ps, 1)
            pe.wait_ge(s_bS_done, 1)
            pe.wait_ge(s_wkd_in, 96)
            pe.wait_ge(s_hT_ready, 2 * NT)
            for n in range(NT):
                R = rows_of[n]
                if n >= 4:
                    pe.wait_ge(s_bk_done, n - 3)
                for c in range(KC):
                    last = mm(PB[n % 4][0:R, 0:272], hT[:, c, n * P:n * P + R], wbk[:, c, :], start=c == 0, stop=c == KC - 1)
                last.then_inc(s_bk_ps, 1)
            pe.wait_ge(s_rel_done, 1)
            for v in range(2):
                if v == 0:
                    pe.wait_ge(s_bk_done, NT)
                for c in range(KC):
                    w = wkd[:, c, v, :, :].rearrange("p u d -> p (u d)")
                    mm(PB[4 + v][:, :], w, hT[:, c, 0:TP], start=c == 0, stop=c == KC - 1)
                for c in range(KC):
                    w = wkd[:, c, v, :, :].rearrange("p u d -> p (u d)")
                    last = mm(PB[2 + v][:, 0:TS], w, hT[:, c, TP:T], start=c == 0, stop=c == KC - 1)
                last.then_inc(s_kd_ps, 1)
            pe.wait_ge(s_ba_ready, 3)
            gp = graw[:, 0:NP, :].rearrange("p n h -> p (n h)")
            mm(PB[7][:, 0:32], m_le[:, :], gp, start=True, stop=True)
            mm(PB[7][:, 32:64], ones[:, :], gp, start=True, stop=True)
            mm(PB[7][0:TS, 64:72], s_le[:, :], graw[0:TS, NP, :], start=True, stop=True)
            mm(PB[7][0:TS, 72:80], blk[:, :, :].rearrange("p b l -> p (b l)"), graw[0:TS, NP, :], start=True, stop=True)
            mm(PB[7][:, 80:144], ones[0:TS, :], sS[:, 0, 0:64], start=True, stop=True).then_inc(s_g_ps, 1)
            pe.wait_ge(s_g_ready, 10)
            pe.wait_ge(s_kd_done, 6)
            pe.wait_ge(s_bk_done, NT)

            with pe.Fori(0, H) as h:
                kv = h // 4
                pe.wait_ge(s_cs_in, h * 32 + 32)
                pe.wait_ge(s_sS_done, 1 + h)
                pe.sem_inc(s_pe_passed, 1)
                for g in range(3):
                    last = tr(PB[7][:, g * 28:(g + 1) * 28], cs[0:28, g, :], ident[0:28, 0:28])
                last.then_inc(s_cst_ps, 1)
                pe.wait_ge(s_wch_in, h * 64 + 64)
                pe.wait_ge(s_o_done, 1 + h * NT)
                for g in range(4):
                    for c in range(KC):
                        last = mm(PB[g][:, :], wch[:, c, g, :], hT[:, c, 0:TP], start=c == 0, stop=c == KC - 1)
                    last.then_inc(s_proj_ps, 1)
                    if g == 0:
                        pe.wait_ge(s_mix_done, 1 + h * NT)
                        for k in range(4):
                            for c in range(KC):
                                last = mm(PB[4][:, k * TS:(k + 1) * TS], wch[:, c, k, :], hT[:, c, TP:T], start=c == 0, stop=c == KC - 1)
                        last.then_inc(s_projs_ps, 1)

                def rows(n):
                    R = rows_of[n]
                    if n == 0:
                        pe.wait_ge(s_wrow_in, h * 48 + 48)
                        pe.wait_ge(s_sS_done, 1 + h)
                    else:
                        pe.wait_ge(s_rows_done, 1 + h * NT + (n - 1))
                    for c in range(KC):
                        last = mm(PB[5 + n % 2][0:R, 0:3 * P], hT[:, c, n * P:n * P + R], wrow[:, c, :, :].rearrange("p g k -> p (g k)"),
                                  start=c == 0, stop=c == KC - 1)
                    last.then_inc(s_rows_ps, 1)

                def each(bank, lhs, rhs, start=True, stop=True):
                    for n in range(NP):
                        last = mm(PB[bank][:, n * P:(n + 1) * P], lhs[:, n, :], rhs[:, n, :], start=start, stop=stop)
                    return last

                qT = qk[:, 0, 0:TP].rearrange("p (n k) -> p n k", n=NP)
                kT = qk[:, 1, 0:TP].rearrange("p (n k) -> p n k", n=NP)
                rows(0)
                pe.wait_ge(s_gm_ready, h * 2 + 2)
                pe.wait_ge(s_cst_ready, h + 1)
                for n in range(NP):
                    last = mm(PB[7][:, n * P:(n + 1) * P], gm[:, n, :], m_gt[:, :], start=True, stop=True)
                last.then_inc(s_D_ps, 1)
                rows(1)
                pe.wait_ge(s_ct_ready, h + 1)
                for g in range(3):
                    last = tr(PB[4][0:27, P + g * P:2 * P + g * P], ct[:, g, :], ident[:, :])
                last.then_inc(s_ct_ps, 1)
                pe.wait_ge(s_sq_done, h + 1)
                pe.wait_ge(s_raw_done, h * 7 + 7)
                pe.wait_ge(s_crow_ready, h + 1)
                for g in range(2):
                    mm(PB[g][:, :], ones[:, :], ex[:, g, 0:TP], start=True, stop=True)
                mm(PB[4][:, 0:64], ones[:, :], ex[:, 0:2, TP:T], start=True, stop=True).then_inc(s_nrm_ps, 1)
                rows(2)
                pe.wait_ge(s_co_done, h * 3 + 3)
                for n in range(NP):
                    last = tr(PB[3][:, n * P:(n + 1) * P], co[:, 2, n * P:(n + 1) * P], ident[:, :])
                last.then_inc(s_vr_ps, 1)
                pe.wait_ge(s_Em_ready, h * 2 + 2)
                for n in range(NP):
                    last = tr(PB[7][:, n * P:(n + 1) * P], E[:, n, :], ident[:, :])
                last.then_inc(s_Et_ps, 1)
                rows(3)
                pe.wait_ge(s_qk_done, h + 1)
                each(0, kT, kT).then_inc(s_kk_ps, 1)
                each(1, kT, qT).then_inc(s_kq_ps, 1)
                for n in range(NP):
                    last = tr(PB[2][:, n * P:(n + 1) * P], kT[:, n, :], ident[:, :])
                last.then_inc(s_kr_ps, 1)
                rows(4)
                pe.wait_ge(s_N_done, h + 1)
                pe.wait_ge(s_kvr_done, h * 3 + 1)
                for n in range(NP):
                    last = tr(PB[3][:, n * P:(n + 1) * P], PW[:, 0, n, :], ident[:, :])
                last.then_inc(s_Nt_ps, 1)
                qs_, ks_ = qk[:, 0, TP:T], qk[:, 1, TP:T]
                b6 = PB[6]
                pe.wait_ge(s_rows_done, 1 + h * NT + 4)
                tr(b6[0:TS, 224:352], ks_, ident[:, :])
                tr(b6[0:TS, 352:480], co[:, 2, TP:T], ident[:, :]).then_inc(s_smp_ps, 1)
                mm(b6[0:TS, 0:TS], sS[:, 8, 0:TS], s_gt[:, :], start=True, stop=True).then_inc(s_smp_ps, 1)

                def square(k):
                    if k == 1:
                        pe.wait_ge(s_Nt_done, h + 1)
                        pe.wait_ge(s_attn_done, h + 1)
                    else:
                        pe.wait_ge(s_ev_p, h * LV + (k - 1))
                        pe.wait_ge(s_ev_pt, h * (LV - 1) + (k - 1))
                    a = (k - 1) % 2
                    each(0, PT[:, a, :, :], PW[:, a, :, :]).then_inc(s_lev_p, 1)
                    if k < LV:
                        each(1, PW[:, a, :, :], PT[:, a, :, :]).then_inc(s_lev_pt, 1)

                def grow(k):
                    pe.wait_ge(s_ev_p, h * LV + k)
                    if k == 1:
                        pe.wait_ge(s_Tt0_done, h + 1)
                        pe.wait_ge(s_kvr_done, h * 3 + 3)
                    else:
                        pe.wait_ge(s_ev_t, h * LV + (k - 1))
                    each(2, PW[:, k % 2, :, :], Tt).then_inc(s_lev_t, 1)

                def scores(n):
                    lo = P if n == 0 else 0
                    if n == 0:
                        pe.wait_ge(s_Et_done, h + 1)
                    elif n == 1:
                        pe.wait_ge(s_rows_done, 1 + h * NT + NT)
                    else:
                        pe.wait_ge(s_sc_add, h * NP + (n - 1))
                    bank = PB[7 if n % 2 == 0 else 5]
                    for u in range(2):
                        last = mm(bank[:, u * 256 + lo:(u + 1) * 256], sqT[:, n * P:(n + 1) * P],
                                  kz[:, u, ds(kv), (n - 1) * P + lo:(n + 1) * P].rearrange("p a k -> p (a k)"), start=True, stop=True)
                    last.then_inc(s_sc_ps, 1)

                def turn_p(n):
                    lo = 1 if n == 0 else 0
                    pe.wait_ge(s_p_exp, h * 3 * NP + 3 * (n + 1))
                    if n == 0:
                        pe.wait_ge(s_Nt_done, h + 1)
                        pe.wait_ge(s_Tt0_done, h + 1)
                    else:
                        pe.wait_ge(s_pt_done, h * NP + n)
                    j = 0
                    for u in range(2):
                        for s in range(lo, 2):
                            last = tr(PB[3][:, j * P:(j + 1) * P], sm[:, n % 2, u, s * P:(s + 1) * P], ident[:, :])
                            j += 1
                    last.then_inc(s_pt_ps, 1)

                def pv(n):
                    lo = 1 if n == 0 else 0
                    pe.wait_ge(s_pt_done, h * NP + (n + 1))
                    if n == 0:
                        pe.wait_ge(s_crow_ready, h + 1)
                        pe.wait_ge(s_rn_done, h * 2 + 2)
                    j = 0
                    for u in range(2):
                        for s in range(lo, 2):
                            last = mm(PB[4][:, n * P + u * HD:n * P + (u + 1) * HD], pT[:, j, :],
                                      kvrow[:, n - 1 + s, ds(kv * HD + 2 * HD, HD)], start=s == lo, stop=s == 1)
                            j += 1
                    last.then_inc(s_pv_ps, 1)

                square(1)
                pe.wait_ge(s_gm_ready, h * 2 + 2)
                pe.wait_ge(s_smp_done, h * 13 + 5)
                pe.wait_ge(s_smp_done, h * 13 + 3)
                pe.sem_inc(s_pe_passed, 1)
                mm(b6[0:TS, 32:64], ks_, ks_, start=True, stop=True)
                mm(b6[0:TS, 64:96], ks_, qs_, start=True, stop=True)
                tr(b6[0:TS, 96:128], sS[:, 3, 32:64], ident[0:TS, 0:TS]).then_inc(s_smp_ps, 1)
                scores(0)
                square(2)
                grow(1)
                pe.wait_ge(s_smp_done, h * 13 + 8)
                pe.sem_inc(s_pe_passed, 1)
                tr(b6[0:TS, 128:160], sS[:, 4, 0:TS], ident[0:TS, 0:TS]).then_inc(s_smp_ps, 1)
                scores(1)
                turn_p(0)
                square(3)
                grow(2)
                pe.wait_ge(s_smp_done, h * 13 + 10)
                pe.sem_inc(s_pe_passed, 1)
                mm(b6[0:TS, 160:192], sS[:, 5, 0:TS], sS[:, 4, 0:TS], start=True, stop=True).then_inc(s_smp_ps, 1)
                scores(2)
                pv(0)
                turn_p(1)
                square(4)
                grow(3)
                pe.wait_ge(s_smp_done, h * 13 + 11)
                pe.sem_inc(s_pe_passed, 1)
                mm(b6[0:TS, 192:224], sS[:, 5, 64:96], sS[:, 5, 32:64], start=True, stop=True).then_inc(s_smp_ps, 1)
                scores(3)
                pv(1)
                turn_p(2)
                square(5)
                grow(4)
                pe.wait_ge(s_smp_done, h * 13 + 12)
                pe.wait_ge(s_smp_done, h * 13 + 3)
                mm(b6[:, 480:512], sS[:, 1, :], sS[:, 5, 96:128], start=True, stop=True).then_inc(s_smp_ps, 1)
                pv(2)
                turn_p(3)
                square(6)
                grow(5)
                pv(3)
                pe.wait_ge(s_sW_done, h * 3 + 2)
                pe.wait_ge(s_st_in, h * 16 + 16)
                for b in range(B):
                    last = mm(b6[:, b * 2 * L:(b + 1) * 2 * L], Sb[:, b, :], wqT[:, b, :, :].rearrange("p a l -> p (a l)"), start=True, stop=True)
                last.then_inc(s_smp_ps, 1)
                grow(6)
                pe.wait_ge(s_smp_done, h * 13 + 13)
                pe.sem_inc(s_pe_passed, 1)
                mm(b6[0:TS, 64:192], sS[:, 5, 96:128], sS[:, 0, :], start=True, stop=False)
                mm(b6[0:TS, 64:192], wqo[:, 0, :], ident[:, :], start=False, stop=True)
                mm(b6[0:TS, 192:320], wqo[:, 1, :], ident[:, :], start=True, stop=True).then_inc(s_smp_ps, 1)
                pe.wait_ge(s_ev_t, h * LV + LV)
                pe.wait_ge(s_pt_done, h * NP + NP)
                each(3, Rk, Tt).then_inc(s_wT_ps, 1)
                for n in range(NP):
                    o = slice(n * P, (n + 1) * P)
                    if n:
                        pe.wait_ge(s_S_done, h * NP + n)
                    last = mm(PB[0][:, o], Tt[:, n, :], Rv[:, n, :], start=True, stop=n == 0)
                    if n:
                        mm(PB[0][:, o], nwT[:, n, :], St, start=False, stop=True).then_inc(s_vn_ps, 1)
                        pe.wait_ge(s_o_done, 1 + h * NT + n)
                        mm(PB[1][:, o], qT[:, n, :], St, start=True, stop=True)
                    else:
                        last.then_inc(s_vn_ps, 1)
                        pe.wait_ge(s_wT_done, h + 1)
                    pe.wait_ge(s_vn_done, h * NP + (n + 1))
                    mm(PB[3][:, o], kd[:, n, :], vnew[:, n, :], start=True, stop=True).then_inc(s_sn_ps, 1)
                    mm(PB[2][:, o], attn[:, n, :], vnew[:, n, :], start=True, stop=True).then_inc(s_o_ps, 1)
                    if n == 2:
                        pe.wait_ge(s_sW_done, h * 3 + 3)
                        pe.sem_inc(s_pe_passed, 1)
                        mm(b6[0:TS, 320:448], sS[:, 4, 64:96], sS[:, 6, :], start=True, stop=True).then_inc(s_smp_ps, 1)
                pe.wait_ge(s_Vm_done, h + 1)
                pe.wait_ge(s_sc_add, h * NP + NP)
                for k in range(2):
                    last = mm(PB[5 + 2 * k][:, :], sS[:, 2, :], Vm[:, 4 * k:4 * k + 4, :].rearrange("p b k -> p (b k)"), start=True, stop=True)
                last.then_inc(s_smp_ps, 1)

            pe.wait_ge(s_mix_done, 1 + H * NT)
            pe.wait_ge(s_sS_done, 1 + H)
            pe.wait_ge(s_keys_in, 64)
            for k in range(4):
                for i in range(4):
                    unit = 4 * k + i
                    last = tr(PB[k][:, i * P:(i + 1) * P], krows[:, unit // 2, unit % 2, :, :].rearrange("p u d -> p (u d)"), ident[:, :])
                last.then_inc(s_att_ps, 1)
            pe.wait_ge(s_att_act, 4)
            pe.wait_ge(s_att_dve, 1)
            for g in range(4):
                for j in range(4):
                    b, v = (g // 2) * 4 + j, g % 2
                    last = mm(PB[4 + g][32 * j:32 * j + 32, 0:P + L], qz[:, b, v, :, :].rearrange("p u k -> p (u k)"), kS[:, 2 * b + v, :], start=True, stop=True)
            last.then_inc(s_att_ps, 1)
            pe.wait_ge(s_att_dve, 3)
            for g in range(4):
                tr(PB[0][:, g * P:(g + 1) * P], pS[:, g, 0:P], ident[:, :])
            for g in range(4):
                last = tr(PB[1][0:L, g * P:(g + 1) * P], pS[:, g, P:], ident[:, :])
            last.then_inc(s_att_ps, 1)
            pe.wait_ge(s_cache_in, 16 * (1 + B))
            pe.wait_ge(s_att_act, 8)
            for g in range(4):
                for j in range(4):
                    b, v = (g // 2) * 4 + j, g % 2
                    o = PB[2][0:HD, (2 * b + v) * 32:(2 * b + v + 1) * 32]
                    mm(o, vrows[:, b, v * HD:(v + 1) * HD], pTs[:, g, 32 * j:32 * j + 32], start=True, stop=False)
                    last = mm(o, v4[0:L, b, v * HD:(v + 1) * HD], pT4[0:L, g, 32 * j:32 * j + 32], start=False, stop=True)
            last.then_inc(s_att_ps, 1)
            pe.wait_ge(s_att_act, 12)
            for hh in range(SH):
                last = tr(PB[5 + hh // 8][0:TS, (hh % 8) * HD:(hh % 8 + 1) * HD], oT[0:HD, hh, :], ident[0:HD, 0:HD])
            last.then_inc(s_att_ps, 1)
            for n in range(NT):
                R = rows_of[n]
                if n == NP:
                    pe.wait_ge(s_att_dve, 4)
                if n >= 2:
                    pe.wait_ge(s_hT_ready, 2 * NT + (n - 1))
                    pe.wait_ge(s_mT_act, n - 1)
                for q in range(2):
                    for c in range(4):
                        last = tr(PB[2 * (n % 2) + q][:, c * P:c * P + R], mixed[0:R, n, 4 * q + c:D:KC], ident[0:R, 0:R])
                    last.then_inc(s_hT_ps, 1)
            pe.wait_ge(s_hT_ready, 2 * NT + (NT))
            pe.wait_ge(s_mT_act, NT)
            pe.wait_ge(s_keys_in, 64 + 16)

            def out_rows(n):
                R = rows_of[n]
                if n >= 2:
                    pe.wait_ge(s_x2_done, n - 1)
                for q in range(2):
                    for c in range(KC):
                        last = mm(PB[2 * (n % 2) + q][0:R, :], hT[:, c, n * P:n * P + R], wo[:, c, q * 512:(q + 1) * 512], start=c == 0, stop=c == KC - 1)
                last.then_inc(s_y2_ps, 1)

            def route_rows(n):
                R = rows_of[n]
                pe.wait_ge(s_h2_ready, n + 1)
                if n == 0:
                    pe.wait_ge(s_tail_in, 16 * 7)
                if n:
                    pe.wait_ge(s_h2T_done, 2 * n)
                for q in range(2):
                    for c in range(4):
                        last = tr(PB[6 + q][:, c * P:c * P + R], h2r[0:R, n % 2, 4 * q + c:D:KC], ident[0:R, 0:R])
                    last.then_inc(s_h2T_ps, 1)
                pe.wait_ge(s_h2T_done, 2 * n + 2)
                if n:
                    pe.wait_ge(s_lg_done, n)
                for c in range(KC):
                    last = mm(PB[5][0:R, 0:72], h2T[:, n % 2, c, 0:R], wr[:, c, :], start=c == 0, stop=c == KC - 1)
                last.then_inc(s_lg_ps, 1)

            for n in range(NT):
                out_rows(n)
                if n:
                    route_rows(n - 1)
            route_rows(NT - 1)
            pe.wait_ge(s_mlt_done, 1)
            pe.wait_ge(s_e_dif, 2)
            for n in range(NT):
                for m in range(n + 1):
                    mm(PB[0][:, n * 64:(n + 1) * 64], m_lt if m == n else ones[:, :], M[:, m, 2, :], start=m == 0, stop=m == n)
            for m in range(NT):
                last = mm(PB[0][:, NT * 64:(NT + 1) * 64], ones[:, :], M[:, m, 2, :], start=m == 0, stop=m == NT - 1)
            last.then_inc(s_rk_ps, 1)
            pe.wait_ge(s_route_done, 1)

            half = (slice(0, CAP), slice(CAP, P))

            def turn_x(it, a):
                j = it * 2 + a
                pe.wait_ge(X_in[a], it * 16 + 16)
                pe.wait_ge(s_xt_done, 1 + j * 2)
                for q in range(2):
                    for c in range(4):
                        last = tr(PB[q][:, c * P:(c + 1) * P], X[:, a, 4 * q + c:D:KC], ident[:, :])
                    last.then_inc(s_xt_ps, 1)

            def gate_up(it, a, c0, c1):
                j = it * 2 + a
                if c0 == 0:
                    pe.wait_ge(s_xt_done, 1 + j * 2 + 2)
                    pe.wait_ge(gu_in[a], it * 64 + 64)
                for c in range(c0, c1):
                    for k in range(2):
                        last = mm(gu_bank[a][half[k], :], xT[:, a, c, half[k]], wgu[a][:, k, c, :], start=c == 0, stop=c == KC - 1)
                if c1 == KC:
                    last.then_inc(s_gu_ps, 1)

            def turn_hid(it, a):
                j = it * 2 + a
                pe.wait_ge(s_hid_done, j + 1)
                for c in range(FE // P):
                    last = tr(PB[3][:, c * P:(c + 1) * P], hid[:, a, c:FE:FE // P], ident[:, :])
                last.then_inc(s_hT2_ps, 1)

            def down(it, a):
                j = it * 2 + a
                pe.wait_ge(s_hT2_done, j + 1)
                pe.wait_ge(dn_in[a], it * 32 + 32)
                pe.wait_ge(s_ye_a, 1 + j)
                pe.wait_ge(s_ye_v, 1 + j)
                for q in range(2):
                    for c in range(FE // P):
                        for k in range(2):
                            last = mm(PB[4 + q][half[k], :], hidT[:, a, c, half[k]], wdn[a][:, k, c, q * 512:(q + 1) * 512],
                                      start=c == 0, stop=c == FE // P - 1)
                last.then_inc(s_dn_ps, 1)

            def overlapped(it, a, turn=True):
                gate_up(*later(it, a, 1), 0, KC // 2)
                turn_hid(it, a)
                gate_up(*later(it, a, 1), KC // 2, KC)
                if turn:
                    turn_x(*later(it, a, 2))
                down(it, a)

            turn_x(0, 0)
            gate_up(0, 0, 0, KC)
            turn_x(0, 1)
            with pe.Fori(0, NPAIR // 2 - 1) as it:
                for a in range(2):
                    overlapped(it, a)
            overlapped(NPAIR // 2 - 1, 0, turn=False)
            turn_hid(NPAIR // 2 - 1, 1)
            down(NPAIR // 2 - 1, 1)

            def further(it, a, k):
                turn_x(it, a)
                gate_up(it, a, 0, KC)
                turn_hid(it, a)
                down(it, a)

            further_blocks(pe, further)

        @block.vector
        def _(dve):
            ch = Chain(dve, s_dve_own)
            step = ch.step
            tt, ts, stt, cp = dve.tensor_tensor, dve.tensor_scalar, dve.scalar_tensor_tensor, dve.tensor_copy
            dve.memset(rtab[32:33, :], 1.0).then_inc(s_rtab_set, 1)
            dve.wait_ge(s_x_in, 48)
            for n in range(NT):
                R = rows_of[n]
                for q in range(2):
                    dve.wait_ge(s_hT_ps, 2 * n + q + 1)
                    tt(hT[:, 4 * q:4 * q + 4, n * P:n * P + R], PB[2 * (n % 2) + q][:, :].rearrange("p (c k) -> p c k", c=4)[:, :, 0:R],
                       nmix[:, 4 * q:4 * q + 4].unsqueeze(2).to_broadcast([P, 4, R]), ALU.mult).then_inc(s_hT_ready, 1)
            dve.wait_ge(s_rtab_set, 1)
            dve.wait_ge(s_rel_in, 48)
            dve.wait_ge(s_zi_done, 3)
            rt4 = rtab.rearrange("p (v k u) -> p v u k", v=2, u=2)
            for v in range(2):
                for l in range(L):
                    for u in range(2):
                        cp(ltab[:, v, l, :].rearrange("p (j u k l) -> p j u k l", j=4, u=2, k=4)[:, :, u, :, l],
                           rt4[:, v, u, :].unsqueeze(1).to_broadcast([34, 4, 4])).then_inc(s_lt_done, 1)
            dve.wait_ge(s_rel_ps, 2)
            cp(biasS[:, :, :], PB[5][:, 0:266].rearrange("p (v k) -> p v k", v=2)).then_inc(s_bS_done, 1)
            dve.wait_ge(s_setup, 3)
            for n in range(NT):
                R = rows_of[n]
                dve.wait_ge(s_bk_ps, n + 1)
                ch.inc(cp(ba[0:R, n, :], PB[n % 4][0:R, 0:2 * H]))
                cp(kvrow[0:R, n, :], PB[n % 4][0:R, 2 * H:272]).then_inc(s_bk_done, 1)
            g8 = lambda k: tmp[:, 40 * k:40 * k + 40].rearrange("p (n h) -> p n h", n=NT)
            dve.wait_ge(s_small_in, 64)
            dve.wait_ge(s_dve_own, ch.value())
            step(tt(ba[:, :, H:], ba[:, :, H:], dtb.unsqueeze(1).to_broadcast([P, NT, H]), ALU.add))
            stt(g8(1), ba[:, :, H:], -1.0, ba[:, :, H:], ALU.mult, ALU.max).then_inc(s_ba_ready, 1)
            dve.wait_ge(s_g_ready, 3)
            step(ts(g8(0), g8(0), 1.0, None, ALU.add))
            ts(g8(2), g8(2), 1.0, None, ALU.add).then_inc(s_ba_ready, 1)
            step(dve.reciprocal(scal[:, 0, :, :], g8(0)))
            ch.inc(ts(scal[:, 1, :, :], scal[:, 0, :, :], -1.0, None, ALU.mult))
            step(ts(g8(3), ba[:, :, H:], 0.0, None, ALU.max))
            dve.wait_ge(s_g_ready, 4)
            step(tt(g8(3), g8(3), g8(2), ALU.add))
            step(stt(graw, g8(3), -1.0, tmp[:, 160:168].unsqueeze(1).to_broadcast([P, NT, H]), ALU.mult, ALU.mult))
            tt(sS[:, 0, 0:64].rearrange("p (b h) -> p b h", b=B), graw[0:TS, NP, :].unsqueeze(1).to_broadcast([TS, B, H]),
               bsel[:, :].unsqueeze(2).to_broadcast([TS, B, H]), ALU.mult).then_inc(s_ba_ready, 1)
            dve.wait_ge(s_g_ps, 1)
            b7 = PB[7]
            gs = tmp[:, 280:424]
            cp(gs[:, 0:64], b7[:, 0:64]).then_inc(s_ba_ready, 1)
            cp(gs[0:TS, 64:80], b7[0:TS, 64:80]).then_inc(s_ba_ready, 1)
            cp(gs[:, 80:144], b7[:, 80:144]).then_inc(s_ba_ready, 1)
            dve.wait_ge(s_ba_ready, 6)
            ch.inc(tt(tmp[:, 200:232], gs[:, 32:64], gs[:, 0:32], ALU.subtract))
            step(tt(tmp[0:TS, 232:240], gs[0:TS, 72:80], gs[0:TS, 64:72], ALU.subtract))
            ch.inc(ts(tmp[:, 200:232], tmp[:, 200:232], 0.0, None, ALU.min))
            ts(tmp[0:TS, 232:240], tmp[0:TS, 232:240], 0.0, None, ALU.min).then_inc(s_ba_ready, 1)
            dve.wait_ge(s_dve_own, ch.value())
            dve.wait_ge(s_g_ready, 10)
            step(tt(scal[:, 2, :, :], scal[:, 0, :, :], scal[:, 3, :, :], ALU.mult))
            dve.wait_ge(s_bias_in, 48)
            dve.wait_ge(s_slots_moved, 16)
            KD = 91
            with dve.Fori(0, H) as h:
                ch.loop(h, KD)
                dve.wait_ge(s_mix_done, 1 + h * NT)
                dve.wait_ge(s_gate_done, 1 + h * NT)
                ch.inc(cp(hsc[:, 1:6, :], scal[:, 1:6, :, ds(h)].rearrange("p a n k -> p a (n k)")))
                ch.inc(cp(hgl, glS[:, :, ds(h)].rearrange("p b k -> p (b k)")))
                cp(hsc[:, 0, :], graw[:, :, ds(h)].rearrange("p n k -> p (n k)")).then_inc(s_hs_ready, 1)
                cp(hbeta[:, :], scal[:, 0, :, ds(h)].rearrange("p n k -> p (n k)")).then_inc(s_hs_ready, 1)
                w = lambda g, i: cst[:, g, 24 + i:25 + i]
                dve.wait_ge(s_cst_ready, h + 1)
                for g in range(3):
                    ch.inc(cp(rawS[:, g, :, 0:3], cst[:, g, 0:24].rearrange("p (b s) -> p b s", b=B)))
                dve.wait_ge(s_dve_own, ch.value())
                cs_ = lambda g: co[:, g, TP:T].rearrange("p (b l) -> p b l", b=B)
                for g in range(3):
                    dve.wait_ge(s_raw_done, h * 7 + (4 if g == 0 else 4 + g))
                    ch.inc(ts(co[:, g, 0:TP], rawP[:, g, 0:TP], w(g, 0), None, ALU.mult))
                    step(ts(cs_(g), rawS[:, g, :, 0:L], w(g, 0), None, ALU.mult))
                    for i in (1, 2):
                        ch.inc(stt(co[:, g, 0:TP], rawP[:, g, i:i + TP], w(g, i), co[:, g, 0:TP], ALU.mult, ALU.add))
                        step(stt(cs_(g), rawS[:, g, :, i:i + L], w(g, i), cs_(g), ALU.mult, ALU.add))
                    ch.inc(stt(co[:, g, 0:TP], rawP[:, g, 3:3 + TP], w(g, 3), co[:, g, 0:TP], ALU.mult, ALU.add))
                    step(stt(cs_(g), rawS[:, g, :, 3:3 + L], w(g, 3), cs_(g), ALU.mult, ALU.add))
                    dve.sem_inc(s_conv_done, 1)
                    if g == 2:
                        for k in range(3):
                            ch.inc(cp(ct[:, k, 0:3], rawP[:, k, TP:TP + 3]))
                        step(cp(ct[:, :, 3:27].rearrange("p g (b l) -> p g b l", b=B), rawS[:, :, :, L:L + 3]))
                        dve.sem_inc(s_ct_ready, 1)
                    dve.wait_ge(s_exp_co, h * 3 + (g + 1))
                    step(ts(ex[:, g, :], ex[:, g, :], 1.0, None, ALU.add))
                    step(dve.reciprocal(ex[:, g, :], ex[:, g, :]))
                    tt(co[:, g, :], co[:, g, :], ex[:, g, :], ALU.mult).then_inc(s_co_done, 1)

                def gate_mul(n):
                    R = rows_of[n]
                    dve.wait_ge(s_rows_exp, h * NT + (n + 1))
                    b = PB[5 + n % 2]
                    s = sig[0:R, n % 2, :, :]
                    step(ts(s, s, 1.0, None, ALU.add))
                    step(dve.reciprocal(gates[0:R, n, :, :], s))
                    tt(gates[0:R, n, 0, :], gates[0:R, n, 0, :], b[0:R, 0:P], ALU.mult).then_inc(s_rows_done, 1)

                gate_mul(0)
                gate_mul(1)
                dve.wait_ge(s_rn_done, h * 2 + 2)
                dve.wait_ge(s_co_done, h * 3 + 3)
                tt(qk, qk, co[:, 0:2, :], ALU.mult).then_inc(s_qk_done, 1)
                bc = lambda k: (hbeta[:, 0:NP] if k == 0 else hsc[:, k, 0:NP]).unsqueeze(2).to_broadcast([P, NP, P])
                v4 = lambda b: PB[b][:, :].rearrange("p (n k) -> p n k", n=NP)
                dve.wait_ge(s_vr_ps, h + 1)
                tt(Rv, v4(3), bc(0), ALU.mult).then_inc(s_kvr_done, 1)
                gate_mul(2)
                dve.wait_ge(s_Em_ready, h * 2 + 2)
                dve.wait_ge(s_kk_ps, h + 1)
                for n in range(NP):
                    last = stt(PW[:, 0, n, :], PB[0][:, n * P:(n + 1) * P], hsc[:, 1, n:n + 1], Es[:, n, :], ALU.mult, ALU.mult)
                last.then_inc(s_N_done, 1)
                dve.wait_ge(s_kq_ps, h + 1)
                dve.wait_ge(s_Et_done, h + 1)
                tt(attn, v4(1), Et, ALU.mult).then_inc(s_attn_done, 1)
                dve.wait_ge(s_kr_ps, h + 1)
                tt(Rk, v4(2), bc(2), ALU.mult).then_inc(s_kvr_done, 1)
                tt(kd, v4(2), bc(4), ALU.mult).then_inc(s_kvr_done, 1)
                gate_mul(3)
                dve.wait_ge(s_Nt_done, h + 1)
                tt(Tt, PT[:, 0, :, :], ident[:, :].unsqueeze(1).to_broadcast([P, NP, P]), ALU.add).then_inc(s_Tt0_done, 1)
                b6 = PB[6]
                dve.wait_ge(s_sE_exp, h + 1)
                sp_ = lambda k: hbeta[0:TS, NP:NT] if k == 0 else hsc[0:TS, k, NP:NT]
                ts(sS[:, 0, :], b6[0:TS, 352:480], sp_(0), None, ALU.mult).then_inc(s_smp_done, 1)
                ts(sS[:, 1, :], b6[0:TS, 224:352], sp_(2), None, ALU.mult).then_inc(s_smp_done, 1)
                ts(sS[:, 2, :], b6[0:TS, 224:352], sp_(4), None, ALU.mult).then_inc(s_smp_done, 1)
                tt(sS[:, 3, 32:64], sS[:, 3, 0:TS], s_ge[:, :], ALU.mult).then_inc(s_smp_done, 1)
                tt(sS[:, 3, 64:96], sS[:, 3, 0:TS], s_gt[:, :], ALU.mult).then_inc(s_smp_done, 1)

                def powt(k):
                    dve.wait_ge(s_lev_pt, h * (LV - 1) + k)
                    cp(PT[:, k % 2, :, :], v4(1)).then_inc(s_ev_pt, 1)

                def growt(k):
                    dve.wait_ge(s_lev_t, h * LV + k)
                    tt(Tt, v4(2), Tt, ALU.add).then_inc(s_ev_t, 1)

                def softmax(n):
                    lo = P if n == 0 else 0
                    a = att[:, n % 2, :]
                    bank = PB[7 if n % 2 == 0 else 5]
                    if n >= 2:
                        dve.wait_ge(s_pt_ps, h * NP + (n - 1))
                        dve.wait_ge(s_p_exp, h * 3 * NP + 3 * (n - 1))
                    dve.wait_ge(s_sc_ps, h * NP + (n + 1))
                    snk = sinkb[:, ds(h * 2, 2)]
                    step(tt(sm[:, n % 2, :, lo:], bank[:, :].rearrange("p (u k) -> p u k", u=2)[:, :, lo:],
                            bias[:, ds(h * 2, 2), lo:], ALU.add))
                    step(dve.tensor_reduce(a[:, 0:2], sm[:, n % 2, :, lo:], AX.X, ALU.max))
                    step(tt(a[:, 0:2], a[:, 0:2], snk, ALU.max))
                    step(ts(a[:, 2:4], a[:, 0:2], -1.0, None, ALU.mult))
                    tt(a[:, 4:6], snk, a[:, 0:2], ALU.subtract).then_inc(s_sc_add, 1)

                def denom(n):
                    a = att[:, n % 2, :]
                    dve.wait_ge(s_p_exp, h * 3 * NP + 3 * (n + 1))
                    step(tt(rinv[:, n, :], a[:, 6:8], esk[:, n % 2, :], ALU.add))
                    ch.inc(dve.reciprocal(rinv[:, n, :], rinv[:, n, :]))

                powt(1)
                gate_mul(4)
                softmax(0)
                dve.wait_ge(s_smp_ps, h * 11 + 3)
                dve.wait_ge(s_smp_done, h * 13 + 5)
                stt(sS[:, 4, 0:TS], b6[0:TS, 32:64], sp_(1), sS[:, 3, 64:96], ALU.mult, ALU.mult).then_inc(s_smp_done, 1)
                cp(sS[:, 4, 32:64], b6[0:TS, 96:128]).then_inc(s_smp_done, 1)
                dve.wait_ge(s_smp_done, h * 13 + 7)
                tt(sS[:, 4, 64:96], b6[0:TS, 64:96], sS[:, 4, 32:64], ALU.mult).then_inc(s_smp_done, 1)
                powt(2)
                growt(1)
                softmax(1)
                denom(0)
                dve.wait_ge(s_smp_ps, h * 11 + 4)
                cp(sS[:, 5, 0:TS], b6[0:TS, 128:160]).then_inc(s_smp_done, 1)
                tt(sS[:, 5, 32:64], b6[0:TS, 128:160], ident[0:TS, 0:TS], ALU.add).then_inc(s_smp_done, 1)
                powt(3)
                growt(2)
                dve.wait_ge(s_smp_ps, h * 11 + 5)
                cp(sS[:, 5, 64:96], b6[0:TS, 160:192]).then_inc(s_smp_done, 1)
                softmax(2)
                denom(1)
                powt(4)
                growt(3)
                dve.wait_ge(s_smp_ps, h * 11 + 6)
                tt(sS[:, 5, 96:128], b6[0:TS, 192:224], sS[:, 5, 32:64], ALU.add).then_inc(s_smp_done, 1)
                softmax(3)
                denom(2)
                powt(5)
                growt(4)
                denom(3)
                growt(5)
                dve.wait_ge(s_smp_ps, h * 11 + 8)
                cp(wqo[:, :, :].rearrange("p a (b l) -> p a b l", b=B), b6[:, 0:64].rearrange("p (b a l) -> p a b l", b=B, a=2)).then_inc(s_smp_done, 1)
                growt(6)
                dve.wait_ge(s_gate_done, 1 + h * NT + NT)
                dve.wait_ge(s_pv_ps, h * NP + NP)
                dve.wait_ge(s_dve_own, ch.value())
                for n in range(NP):
                    for u in range(2):
                        last = stt(gates[:, n, 1, u * HD:(u + 1) * HD], PB[4][:, n * P + u * HD:n * P + (u + 1) * HD],
                                   rinv[:, n, u:u + 1], gates[:, n, 2, u * HD:(u + 1) * HD], ALU.mult, ALU.mult)
                        ch.inc(last)
                for n in range(NP):
                    dve.wait_ge(s_sn_ps, h * NP + (n + 1))
                    o = slice(n * P, (n + 1) * P)
                    if n == 0:
                        dve.wait_ge(s_stored, 1 + h)
                        cp(St, PB[3][:, o]).then_inc(s_S_done, 1)
                    else:
                        dve.wait_ge(s_S_done, h * NP + n)
                        stt(St, St, hsc[:, 5, n:n + 1], PB[3][:, o], ALU.mult, ALU.add).then_inc(s_S_done, 1)
                    dve.wait_ge(s_o_ps, h * NP + (n + 1))
                    if n == 0:
                        cp(orow[:, n, :], PB[2][:, o]).then_inc(s_o_done, 1)
                    else:
                        step(ts(orow[:, n, :], PB[1][:, o], hsc[:, 3, n:n + 1], None, ALU.mult))
                        tt(orow[:, n, :], orow[:, n, :], PB[2][:, o], ALU.add).then_inc(s_o_done, 1)
                dve.wait_ge(s_smp_ps, h * 11 + 10)
                step(ts(orow[0:TS, NP, :], b6[0:TS, 192:320], hsc[0:TS, 3, NP:NT], None, ALU.mult))
                tt(orow[0:TS, NP, :], orow[0:TS, NP, :], b6[0:TS, 320:448], ALU.add).then_inc(s_o_done, 1)
                dve.wait_ge(s_smp_ps, h * 11 + 11)
                dve.wait_ge(s_decay_done, h + 1)
                ch.inc(tt(Sb[:, 0:4, :], Sb[:, 0:4, :], v4(5), ALU.add))
                tt(Sb[:, 4:8, :], Sb[:, 4:8, :], v4(7), ALU.add).then_inc(s_sS_done, 1)
                dve.wait_ge(s_rstd_done, h * 2 + 2)
                dve.wait_ge(s_dve_own, ch.value())
                for n in range(NT):
                    R = rows_of[n]
                    if n < NP:
                        step(stt(orow[:, n, :], orow[:, n, :], ssq[:, 2, n:n + 1], gates[:, n, 0, :], ALU.mult, ALU.mult))
                        tt(mixed[:, n, ds(h * P, P)], orow[:, n, :], gates[:, n, 1, :], ALU.add).then_inc(s_mix_done, 1)
                    else:
                        ch.inc(cp(sgb_s[0:TS, ds(h * P, P)], gates[0:TS, NP, 2, :]))
                        stt(mixed[0:TS, n, ds(h * P, P)], orow[0:TS, n, :], ssq[0:TS, 2, n:n + 1], gates[0:TS, n, 0, :], ALU.mult, ALU.mult).then_inc(s_mix_done, 1)
            ch.end(H)
            dve.wait_ge(s_mix_done, 1 + H * NT)
            dve.wait_ge(s_stored, 1 + H)
            dve.wait_ge(s_sS_done, 1 + H)
            dve.wait_ge(s_kd_done, 6)
            dve.wait_ge(s_smp_ps, H * 11)
            kS_ = kS.rearrange("p (b v) k -> p b v k", v=2)
            for v in range(2):
                ch.inc(cp(kS_[:, :, v, P:], skd[:, v, :].rearrange("p (b l) -> p b l", b=B)))
            dve.wait_ge(s_dve_own, ch.value())
            dve.sem_inc(s_att_dve, 1)
            dve.wait_ge(s_att_ps, 5)
            for g in range(4):
                ch.inc(tt(pS[:, g, :], PB[4 + g][:, 0:P + L], biasS[:, g % 2, 0:132], ALU.add))
            dve.wait_ge(s_dve_own, ch.value())
            snk = biasS[:, :, 132:133].rearrange("p v k -> p (v k)").unsqueeze(1).to_broadcast([P, 2, 2])
            col = lambda k: aS[:, :, k:k + 1].rearrange("p g k -> p (g k)").rearrange("p (a v) -> p a v", v=2)
            step(dve.tensor_reduce(aS[:, :, 0], pS, AX.X, ALU.max))
            step(tt(col(0), col(0), snk, ALU.max))
            ch.inc(ts(col(1), col(0), -1.0, None, ALU.mult))
            step(tt(col(2), snk, col(0), ALU.subtract))
            dve.sem_inc(s_att_dve, 1)
            dve.wait_ge(s_att_act, 6)
            step(tt(aS[:, :, 5], aS[:, :, 3], aS[:, :, 4], ALU.add))
            step(dve.reciprocal(aS[:, :, 6], aS[:, :, 5]))
            step(tt(pS, pS, aS[:, :, 6:7].to_broadcast([P, 4, P + L]), ALU.mult))
            dve.sem_inc(s_att_dve, 1)
            dve.wait_ge(s_att_ps, 8)
            for q in range(2):
                step(tt(sgb_s[0:TS, q * 512:(q + 1) * 512], sgb_s[0:TS, q * 512:(q + 1) * 512], PB[5 + q][0:TS, :], ALU.mult))
            tt(mixed[0:TS, NP, :], mixed[0:TS, NP, :], sgb_s[0:TS, :], ALU.add).then_inc(s_att_dve, 1)
            for n in range(NT):
                R = rows_of[n]
                dve.wait_ge(s_hT_ps, 2 * NT + (2 * n + 2))
                cp(hT[:, 4:8, n * P:n * P + R], PB[2 * (n % 2) + 1][:, :].rearrange("p (c k) -> p c k", c=4)[:, :, 0:R]).then_inc(s_hT_ready, 1)
            dve.wait_ge(s_tail_in, 16 * 7)
            dve.memset(M[:, NP, :, :], 0.0).then_inc(s_e_dif, 1)
            dve.wait_ge(s_e_dif, 1)

            def resid(n):
                R = rows_of[n]
                dve.wait_ge(s_y2_ps, n + 1)
                for q in range(2):
                    ch.inc(tt(x2[0:R, n, q * 512:(q + 1) * 512], PB[2 * (n % 2) + q][0:R, :], xr[0:R, n, q * 512:(q + 1) * 512], ALU.add))
                dve.wait_ge(s_dve_own, ch.value())
                dve.sem_inc(s_x2_done, 1)
                dve.wait_ge(s_r_exp, n + 1)
                if n >= 2:
                    dve.wait_ge(s_h2T_ps, 2 * (n - 1))
                    dve.wait_ge(s_h2_out, 16 * (n - 1))
                stt(h2r[0:R, n % 2, :], x2[0:R, n, :], rsc[0:R, n, 2:3], nffn[0:R, :], ALU.mult, ALU.mult).then_inc(s_h2_ready, 1)

            def logits(n):
                R = rows_of[n]
                dve.wait_ge(s_h2T_ps, 2 * n + 2)
                if n >= 2:
                    dve.wait_ge(s_lg_ps, n - 1)
                cp(h2T[:, n % 2, 4:8, 0:R], PB[7][:, :].rearrange("p (c k) -> p c k", c=4)[:, :, 0:R]).then_inc(s_h2T_done, 1)
                dve.wait_ge(s_lg_ps, n + 1)
                tt(lg[0:R, n, :], PB[5][0:R, 0:72], brb[0:R, :], ALU.add).then_inc(s_lg_done, 1)

            dve.wait_ge(s_mlt_done, 1)
            iot = e64[:, 0, :]

            def choose(n):
                R = rows_of[n]
                r = rt[0:R, n, :]
                el, pen, ohg = r[:, 64:128], r[:, 16:24], r[:, 24:32]
                dve.wait_ge(s_lg_done, n + 1)
                step(dve.max(g8v[0:R, n, :], lg[0:R, n, 0:8]))
                step(dve.max_index(gnum[0:R, n, :].bitcast(U32), g8v[0:R, n, :], lg[0:R, n, 0:8]))
                step(cp(r[:, 32:33], gnum[0:R, n, 0:1].bitcast(I32)))
                step(ts(ohg, iot[0:R, 0:8], r[:, 32:33], None, ALU.is_equal))
                step(ts(pen, ohg, 1.0, 1.0e30, ALU.subtract, ALU.mult))
                step(tt(el.rearrange("p (g e) -> p g e", g=8), lg[0:R, n, 8:72].rearrange("p (g e) -> p g e", g=8),
                        pen.unsqueeze(2).to_broadcast([R, 8, 8]), ALU.add))
                step(dve.max(el8[0:R, n, :], el))
                step(dve.max_index(enum_[0:R, n, :].bitcast(U32), el8[0:R, n, :], el))
                step(cp(r[:, 34:36], enum_[0:R, n, 0:2].bitcast(I32)))
                for k in range(2):
                    ch.inc(ts(M[0:R, n, k, :], iot[0:R, :], r[:, 34 + k:35 + k], None, ALU.is_equal))
                dve.wait_ge(s_dve_own, ch.value())
                ch.inc(tt(M[0:R, n, 2, :], M[0:R, n, 0, :], M[0:R, n, 1, :], ALU.add))
                ch.inc(ts(rsc[0:R, n, 3:4], g8v[0:R, n, 0:1], -1.0, None, ALU.mult))
                step(tt(rsc[0:R, n, 5:6], el8[0:R, n, 1:2], el8[0:R, n, 0:1], ALU.subtract))
                dve.sem_inc(s_g_max, 1)

            for n in range(NT):
                resid(n)
                logits(n)
                choose(n)
            dve.sem_inc(s_e_dif, 1)
            dve.wait_ge(s_g_exp, NT + 1)
            for n in range(NT):
                R = rows_of[n]
                c = lambda k: rsc[0:R, n, k:k + 1]
                step(stt(c(7), c(6), 1.0, c(4), ALU.add, ALU.mult))
                step(dve.reciprocal(wts[0:R, n, 0:1], c(7)))
                step(tt(wts[0:R, n, 1:2], wts[0:R, n, 0:1], c(6), ALU.mult))
            dve.wait_ge(s_rk_ps, 1)
            cnt, ova, ovb, ov, adj, eb = (e64[:, k, :] for k in range(1, 7))
            step(cp(cnt, PB[0][:, NT * 64:(NT + 1) * 64]))
            step(ts(ov, cnt, float(CAP), None, ALU.is_gt))
            for k in range(2, T // CAP + 1):
                step(stt(ov, cnt, float(CAP * k), ov, ALU.is_gt, ALU.add))
            src, dst = ov, ova
            k = 1
            while k < NE:
                ch.inc(cp(dst[:, 0:k], src[:, 0:k]))
                step(tt(dst[:, k:], src[:, k:], src[:, 0:NE - k], ALU.add))
                src, dst = dst, (ovb if dst is ova else ova)
                k *= 2
            incl, excl = src, dst
            step(tt(excl, incl, ov, ALU.subtract))
            ch.inc(ts(eb, iot, float(CAP), None, ALU.mult))
            step(tt(adj, excl, iot, ALU.subtract))
            step(ts(adj, adj, float(NE - 1), float(CAP), ALU.add, ALU.mult))
            dall = rt.rearrange("p n (k e) -> p n k e", k=6)
            b4 = lambda t: t.unsqueeze(1).to_broadcast([P, NT, 64])
            rk = PB[0][:, 0:NT * 64].rearrange("p (n e) -> p n e", n=NT)
            step(ts(dall[:, :, 0, :], rk, float(CAP), None, ALU.is_ge))
            step(tt(dall[:, :, 0, :], dall[:, :, 0, :], b4(adj), ALU.mult))
            step(tt(dall[:, :, 1, :], rk, b4(eb), ALU.add))
            step(tt(dall[:, :, 0, :], dall[:, :, 0, :], dall[:, :, 1, :], ALU.add))
            for k in range(2):
                for n in range(NT):
                    R = rows_of[n]
                    ch.inc(tt(dall[0:R, n, 2 + k, :], dall[0:R, n, 0, :], M[0:R, n, k, :], ALU.mult))
            dve.wait_ge(s_dve_own, ch.value())
            for n in range(NT):
                R = rows_of[n]
                ch.inc(dve.tensor_reduce(rsc[0:R, n, 8:10], dall[0:R, n, 2:4, :], AX.X, ALU.add))
            dve.wait_ge(s_dve_own, ch.value())
            J = NBLK // 2
            parts = ((P, slice(0, NP)), (TS, slice(NP, NT)))
            past = xr[:, 2, 0:2 * NP * (J - 1)].rearrange("p (n k j) -> p n k j", n=NP, k=2), xr[:, 3, 0:2 * (J - 1)].rearrange("p (n k j) -> p n k j", n=1, k=2)
            for R, n in parts:
                ch.inc(ts(rsc[0:R, n, 10:12], rsc[0:R, n, 8:10], 1.0 / P, None, ALU.mult))
            dve.wait_ge(s_dve_own, ch.value())
            for (R, n), t in zip(parts, past):
                shape = [R, t.shape[1], 2, J - 1]
                ch.inc(tt(t[0:R], rsc[0:R, n, 10:12].unsqueeze(3).to_broadcast(shape),
                          iot[0:R, 1:J].unsqueeze(1).unsqueeze(1).to_broadcast(shape), ALU.is_ge))
            dve.wait_ge(s_dve_own, ch.value())
            for (R, n), t in zip(parts, past):
                ch.inc(dve.tensor_reduce(rsc[0:R, n, 12:14], t[0:R], AX.X, ALU.add))
                ch.inc(ts(rsc[0:R, n, 8:10], rsc[0:R, n, 8:10], float(J), None, ALU.mult))
            dve.wait_ge(s_dve_own, ch.value())
            for R, n in parts:
                ch.inc(ts(rsc[0:R, n, 12:14], rsc[0:R, n, 12:14], float(1 - P * J), None, ALU.mult))
            dve.wait_ge(s_dve_own, ch.value())
            for R, n in parts:
                ch.inc(tt(dsti[0:R, n, :], rsc[0:R, n, 8:10], rsc[0:R, n, 12:14], ALU.add))
            dve.wait_ge(s_dve_own, ch.value())
            dve.sem_inc(s_M_done, 1)
            bb = lambda t: t[0:1, :].unsqueeze(1).to_broadcast([1, OV, 64])
            w1, w2 = (xr[0:1, k, :].rearrange("p (b e) -> p b e", b=OV) for k in range(2))
            ch.inc(tt(w1, i16[0:1, :, :], bb(excl), ALU.is_ge))
            step(tt(w2, i16[0:1, :, :], bb(incl), ALU.is_lt))
            step(tt(w1, w1, w2, ALU.mult))
            step(tt(w1, w1, bb(iot), ALU.mult))
            step(dve.tensor_reduce(rsc[0:1, 1, 0:16], w1, AX.X, ALU.add))
            ch.inc(cp(ovt[0:1, 0:OV], rsc[0:1, 1, 0:16]))
            step(cp(ovt[0:1, OV:OV + 1], incl[0:1, NE - 1:NE]))
            dve.sem_inc(s_ov_done, 1)
            dve.wait_ge(s_act_own, 1)
            dve.sem_inc(s_route_done, 1)

            def turned(it, a):
                j = it * 2 + a
                dve.wait_ge(s_xt_ps, 3 + j * 2 + 2)
                cp(xT[:, a, 4:8, :], PB[1][:, :].rearrange("p (c k) -> p c k", c=4)).then_inc(s_xt_done, 1)

            def silu(it, a):
                j = it * 2 + a
                dve.wait_ge(s_hg_exp, j + 1)
                ts(hb[:, a, :], hb[:, a, :], 1.0, None, ALU.add).then_inc(s_hid_own, 1)
                dve.wait_ge(s_hid_own, j * 3 + 1)
                dve.reciprocal(hb[:, a, :], hb[:, a, :]).then_inc(s_hid_own, 1)
                dve.wait_ge(s_hid_own, j * 3 + 2)
                tt(hid[:, a, :], hb[:, a, :], gu_bank[a][:, 0:FE], ALU.mult).then_inc(s_hid_own, 1)
                dve.wait_ge(s_hid_own, j * 3 + 3)
                tt(hid[:, a, :], hid[:, a, :], gu_bank[a][:, FE:], ALU.mult).then_inc(s_hid_done, 1)

            def rows_out(it, a):
                j = it * 2 + a
                dve.wait_ge(s_dn_ps, 2 + j + 1)
                dve.wait_ge(ye_out[a], 1 + it * 16)
                cp(ys[:, a, 512:], PB[5][:, :]).then_inc(s_ye_v, 1)

            def follow(it, a, nxt=True, turn=True):
                if nxt:
                    silu(*later(it, a, 1))
                if turn:
                    turned(*later(it, a, 2))
                rows_out(it, a)

            turned(0, 0)
            silu(0, 0)
            turned(0, 1)
            with dve.Fori(0, NPAIR // 2 - 1) as it:
                for a in range(2):
                    follow(it, a)
            follow(NPAIR // 2 - 1, 0, turn=False)
            follow(NPAIR // 2 - 1, 1, nxt=False, turn=False)

            def further(it, a, k):
                turned(it, a)
                silu(it, a)
                rows_out(it, a)

            further_blocks(dve, further)
            dve.wait_ge(s_fin_in, 16)
            def weigh(n):
                R = rows_of[n]
                dve.wait_ge(yg_in[n % 2], 32 * (n // 2 + 1))
                step(stt(x2[0:R, n, :], yg[0:R, n % 2, 0, :], wts[0:R, n, 0:1], x2[0:R, n, :], ALU.mult, ALU.add))
                stt(x2[0:R, n, :], yg[0:R, n % 2, 1, :], wts[0:R, n, 1:2], x2[0:R, n, :], ALU.mult, ALU.add).then_inc(s_yo_acc, 1)

            def norm_out(n):
                R = rows_of[n]
                dve.wait_ge(s_r_exp, NT + n + 1)
                if n >= 2:
                    dve.wait_ge(s_yo_out, 16 * (n - 1))
                stt(yo[0:R, n % 2, :], x2[0:R, n, :], sc[0:R, 16 + n:17 + n], nfin[0:R, :], ALU.mult, ALU.mult).then_inc(s_yo_fin, 1)

            for n in range(NT):
                weigh(n)
                if n:
                    norm_out(n - 1)
            norm_out(NT - 1)


def kernel(**inputs):
    import numpy as np
    from concourse import bacc
    from concourse.bass_utils import run_bass_kernel_spmd

    nc = bacc.Bacc("TRN2", target_bir_lowering=False, num_devices=1)
    arrays, aps = {}, {}
    for name, a in inputs.items():
        a = np.ascontiguousarray(a)
        arrays[f"in_{name}"] = a
        aps[name] = nc.dram_tensor(f"in_{name}", a.shape, mybir.dt.from_np(a.dtype), kind="ExternalInput").ap()
    n = 255 - np.arange(384)
    far = 16 + (np.log(np.maximum(n, 1).astype(np.float32) / 16) / np.log(8.0) * 16).astype(np.int32)
    bucket = np.where(n < 16, n, np.minimum(far, 31))
    inside = (n >= 0) & (n < 128)
    rel = np.zeros((34, 385), np.float32)
    rel[33, 384] = 1.0
    for j in range(384):
        if inside[j]:
            rel[bucket[j], j] = 1.0
        else:
            rel[32, j] = NEG
    arrays["in_rel_map"] = rel
    rel_ap = nc.dram_tensor("in_rel_map", rel.shape, F32, kind="ExternalInput").ap()

    shapes = [(1, 512, 1024), (8, 4, 1024), (1, 1, 3, 3072), (1, 1, 8, 128, 128), (1, 1, 128, 2, 64), (1, 1, 128, 2, 64),
              (1, 8, 3, 3072), (1, 8, 8, 128, 128), (1, 8, 128, 2, 64), (1, 8, 128, 2, 64)]
    outs = [nc.dram_tensor(f"out_{i}", s, F32, kind="ExternalOutput").ap() for i, s in enumerate(shapes)]
    a = aps
    flat = lambda t: t.rearrange("a b -> (a b)")
    one = lambda t: t[0]
    program(nc, a["x_prompt"][0], a["x_sample"].rearrange("b l d -> (b l) d"), a["state_dn_conv"][0], a["state_dn"][0],
            a["cache_swa_k"][0].rearrange("b s g d -> b s (g d)"), a["cache_swa_v"][0].rearrange("b s g d -> b s (g d)"),
            a["w_in"][0], a["conv_w"][0], a["a_log"][0], a["dt_bias"][0], a["dn_norm_w"][0], a["sinks"][0], a["rel_bias"],
            a["w_out"][0], a["norm_mix_w"][0], a["norm_ffn_w"][0], a["w_router_group"][0], a["b_router_group"][0],
            a["w_router_expert"][0], a["b_router_expert"][0], a["w_gate"][0], a["w_up"][0], a["w_down"][0],
            a["norm_final_w"], rel_ap,
            outs[0][0], outs[1].rearrange("b l d -> (b l) d"), outs[2][0, 0].rearrange("s (g k) -> s g k", g=3), outs[3][0, 0],
            outs[4][0, 0].rearrange("s g d -> s (g d)"), outs[5][0, 0].rearrange("s g d -> s (g d)"),
            outs[6][0].rearrange("b s (g k) -> (b s) g k", g=3), outs[7][0],
            outs[8][0].rearrange("b s g d -> b s (g d)"), outs[9][0].rearrange("b s g d -> b s (g d)"))
    r = run_bass_kernel_spmd(nc, [arrays], core_ids=[0])
    return tuple(r.results[0][f"out_{i}"] for i in range(len(shapes)))
```
